# Optimizing a Trainium2 kernel written in Bass

```python
import math
import jax, jax.numpy as jnp
from jax import lax
import numpy as np

D_MODEL = 1024
BATCH = 1
SEQ = 512
DEPTH = 2

EPS = 1e-6
D_FF = -(-8 * D_MODEL // (3 * 256)) * 256

POOL_WINDOWS = (2, 4, 8, 16)
POOL_WIDTH = D_MODEL // 2
POOL_GROUP = POOL_WIDTH // len(POOL_WINDOWS)

HGRN_HEADS = 4
HGRN_DK = 128
HGRN_DV = (D_MODEL // 2) // HGRN_HEADS
HGRN_CHUNK = 64
HGRN_KW = HGRN_HEADS * HGRN_DK
HGRN_VW = HGRN_HEADS * HGRN_DV

HYB_IN = POOL_WIDTH + 2 * HGRN_KW + 2 * HGRN_VW
HYB_OUT = POOL_WIDTH + HGRN_VW

DIL_GROUPS = ((128, 1), (512, 4), (2048, 16))
ATT_HEADS_PER_GROUP = 8
ATT_HEAD_DIM = 64
ATT_GROUP_WIDTH = ATT_HEADS_PER_GROUP * ATT_HEAD_DIM
N_ATT_HEADS = len(DIL_GROUPS) * ATT_HEADS_PER_GROUP
ATT_QKV = 3 * len(DIL_GROUPS) * ATT_GROUP_WIDTH
ATT_OUT = ATT_GROUP_WIDTH
REL_BUCKETS = 32
REL_MAX_DIST = 2048

N_HYB = (DEPTH + 1) // 2
N_ATT = DEPTH // 2


def rms_norm(x, gain):
    xf = x.astype(jnp.float32)
    y = xf * lax.rsqrt(jnp.mean(xf * xf, axis=-1, keepdims=True) + EPS)
    return (y * gain.astype(jnp.float32)).astype(x.dtype)

def t5_bucket(dist):
    max_exact = REL_BUCKETS // 2
    df = jnp.maximum(dist, 1).astype(jnp.float32)
    large = max_exact + (jnp.log(df / max_exact) / math.log(REL_MAX_DIST / max_exact)
                         * (REL_BUCKETS - max_exact)).astype(jnp.int32)
    large = jnp.minimum(large, REL_BUCKETS - 1)
    return jnp.where(dist < max_exact, dist, large)

def pool_mixer(u, w, scale):
    B, S, _ = u.shape
    uf = u.astype(jnp.float32)
    wmax = max(POOL_WINDOWS)
    cs = jnp.cumsum(uf, axis=1)
    cs_pad = jnp.pad(cs, ((0, 0), (wmax, 0), (0, 0)))
    pos = jnp.arange(S)
    diffs = []
    for gi, win in enumerate(POOL_WINDOWS):
        sl = slice(gi * POOL_GROUP, (gi + 1) * POOL_GROUP)
        window_sum = cs[:, :, sl] - cs_pad[:, wmax - win: wmax - win + S, sl]
        count = jnp.minimum(pos + 1, win).astype(jnp.float32)[None, :, None]
        diffs.append(window_sum / count - uf[:, :, sl])
    d = jnp.stack(diffs, axis=2)
    y = jnp.einsum('bsgc,gcd->bsgd', d, w.astype(jnp.float32)).reshape(B, S, POOL_WIDTH)
    return (y * scale.astype(jnp.float32)).astype(u.dtype)

def hgrn2_mixer(q_raw, f_raw, v_raw, g_raw, lb, out_gain):
    B, S, _ = q_raw.shape
    H, K, V, C = HGRN_HEADS, HGRN_DK, HGRN_DV, HGRN_CHUNK
    n = S // C
    q = jax.nn.silu(q_raw.astype(jnp.float32)).reshape(B, S, H, K)
    z = f_raw.astype(jnp.float32).reshape(B, S, H, K)
    lb = lb.astype(jnp.float32).reshape(H, K)
    log_f = jnp.logaddexp(jnp.log(lb), jnp.log1p(-lb) + jax.nn.log_sigmoid(z))
    k = (1.0 - lb) * jax.nn.sigmoid(-z)
    v = v_raw.astype(jnp.float32).reshape(B, S, H, V)

    def chunks(t):
        return t.reshape(B, n, C, H, t.shape[-1]).transpose(1, 0, 3, 2, 4)

    qc, kc, vc, lfc = chunks(q), chunks(k), chunks(v), chunks(log_f)
    bc = jnp.cumsum(lfc, axis=3)
    causal = jnp.tril(jnp.ones((C, C), dtype=bool))

    def step(state, inp):
        qt, kt, vt, bt = inp
        b_last = bt[:, :, -1:, :]
        o_inter = jnp.einsum('bhtk,bhkv->bhtv', qt * jnp.exp(bt), state)
        rel = jnp.where(causal[:, :, None], bt[:, :, :, None, :] - bt[:, :, None, :, :], -jnp.inf)
        a = jnp.einsum('bhtsk,bhsk->bhts', qt[:, :, :, None, :] * jnp.exp(rel), kt)
        o_intra = jnp.einsum('bhts,bhsv->bhtv', a, vt)
        k_dec = kt * jnp.exp(b_last - bt)
        state = (jnp.exp(b_last[:, :, 0, :, None]) * state
                 + jnp.einsum('bhsk,bhsv->bhkv', k_dec, vt))
        return state, o_inter + o_intra

    state0 = jnp.zeros((B, H, K, V), jnp.float32)
    _, o = lax.scan(step, state0, (qc, kc, vc, bc))
    o = o.transpose(1, 0, 3, 2, 4).reshape(B, S, H, V)
    o = rms_norm(o, out_gain) * jax.nn.silu(g_raw.astype(jnp.float32).reshape(B, S, H, V))
    return o.reshape(B, S, HGRN_VW).astype(q_raw.dtype)

def _to_strided(t, dil, blk):
    B, S, H, E = t.shape
    L = S // dil
    nb = -(-L // blk)
    t = t.reshape(B, L, dil, H, E).transpose(0, 2, 1, 3, 4)
    t = jnp.pad(t, ((0, 0), (0, 0), (0, nb * blk - L), (0, 0), (0, 0)))
    return t.reshape(B, dil, nb, blk, H, E)

def _from_strided(t, S):
    B, dil, nb, blk = t.shape[:4]
    tail = t.shape[4:]
    L = S // dil
    t = t.reshape(B, dil, nb * blk, *tail)[:, :, :L]
    return jnp.moveaxis(t, 1, 2).reshape(B, S, *tail)

def dilated_group_attention(q, k, v, win, dil, bias_table):
    S = q.shape[1]
    blk = win // dil
    qs = _to_strided(q * ATT_HEAD_DIM ** -0.5, dil, blk)
    ks = _to_strided(k, dil, blk)
    vs = _to_strided(v, dil, blk)
    nb = qs.shape[2]

    def with_prev(t):
        prev = jnp.pad(t[:, :, :-1], ((0, 0), (0, 0), (1, 0), (0, 0), (0, 0), (0, 0)))
        return jnp.concatenate([prev, t], axis=3)

    kk, vv = with_prev(ks), with_prev(vs)
    qi = jnp.arange(blk)[:, None]
    ki = jnp.arange(2 * blk)[None, :]
    dist = blk + qi - ki
    band = (dist >= 0) & (dist <= blk)
    bias = bias_table[t5_bucket(jnp.maximum(dist, 0) * dil)].astype(jnp.float32).transpose(2, 0, 1)
    has_prev = (jnp.arange(nb) > 0)[:, None, None] | (ki >= blk)[None]
    mask = band[None] & has_prev
    s = jnp.einsum('brnqhe,brnkhe->brnhqk', qs, kk) + bias
    s = jnp.where(mask[None, None, :, None], s, -jnp.inf)
    m = jnp.max(s, axis=-1, keepdims=True)
    p = jnp.exp(s - m)
    l = jnp.sum(p, axis=-1, keepdims=True)
    mt = jnp.moveaxis(m, 3, 4)
    lt = jnp.moveaxis(l, 3, 4)
    o = jnp.einsum('brnhqk,brnkhe->brnqhe', p, vv) / lt
    return _from_strided(o, S), _from_strided(mt, S), _from_strided(lt, S)

def dilated_attention_mixer(qkv, rel_bias):
    B, S, _ = qkv.shape
    G, Hg = len(DIL_GROUPS), ATT_HEADS_PER_GROUP
    t = qkv.astype(jnp.float32).reshape(B, S, 3, G, Hg, ATT_HEAD_DIM)
    outs, maxes, dens = [], [], []
    for gi, (win, dil) in enumerate(DIL_GROUPS):
        o, m, l = dilated_group_attention(t[:, :, 0, gi], t[:, :, 1, gi], t[:, :, 2, gi], win, dil,
                                          rel_bias[:, gi * Hg:(gi + 1) * Hg])
        outs.append(o)
        maxes.append(m)
        dens.append(l)
    o_all = jnp.stack(outs)
    m_all = jnp.stack(maxes)
    l_all = jnp.stack(dens)
    w = l_all * jnp.exp(m_all - jnp.max(m_all, axis=0, keepdims=True))
    o = jnp.sum(w * o_all, axis=0) / jnp.sum(w, axis=0)
    return o.reshape(B, S, ATT_OUT).astype(qkv.dtype)

def swiglu(h, w_in, w_out):
    a, b = jnp.split(h @ w_in, 2, axis=-1)
    return (jax.nn.silu(a) * b) @ w_out

def modulation(c, w, b):
    return jnp.split(jax.nn.silu(c) @ w + b, 3, axis=-1)

def sandwich(x, mod, g_pre, g_post, fn):
    shift, scale, gate = mod
    h = rms_norm(x, g_pre) * (1.0 + scale[:, None]) + shift[:, None]
    return x + gate[:, None] * rms_norm(fn(h), g_post)

def first_inputs(seed: int = 0) -> dict:
    key = jax.random.key(seed)
    ks = jax.random.split(key, 17)

    def nrm(k, shape, scale):
        return jax.random.normal(k, shape, jnp.float32) * scale

    D = D_MODEL
    return {
        'x': nrm(ks[0], (BATCH, SEQ, D), 1.0),
        'c': nrm(ks[1], (BATCH, D), 1.0),
        'ada_w': nrm(ks[2], (DEPTH, 2, D, 3 * D), D ** -0.5),
        'ada_b': nrm(ks[3], (DEPTH, 2, 3 * D), 0.01),
        'norm_pre': 1.0 + nrm(ks[4], (DEPTH, 2, D), 0.1),
        'norm_post': 1.0 + nrm(ks[5], (DEPTH, 2, D), 0.1),
        'ffn_w_in': nrm(ks[6], (DEPTH, D, 2 * D_FF), D ** -0.5),
        'ffn_w_out': nrm(ks[7], (DEPTH, D_FF, D), D_FF ** -0.5),
        'hyb_w_in': nrm(ks[8], (N_HYB, D, HYB_IN), D ** -0.5),
        'hyb_w_out': nrm(ks[9], (N_HYB, HYB_OUT, D), HYB_OUT ** -0.5),
        'pool_w': nrm(ks[10], (N_HYB, len(POOL_WINDOWS), POOL_GROUP, POOL_GROUP), POOL_GROUP ** -0.5),
        'pool_scale': 1.0 + nrm(ks[11], (N_HYB, POOL_WIDTH), 0.1),
        'hgrn_lb_logits': nrm(ks[12], (N_HYB, HGRN_KW), 1.0),
        'hgrn_out_norm': 1.0 + nrm(ks[13], (N_HYB, HGRN_DV), 0.1),
        'att_w_qkv': nrm(ks[14], (N_ATT, D, ATT_QKV), D ** -0.5),
        'att_w_out': nrm(ks[15], (N_ATT, ATT_OUT, D), ATT_OUT ** -0.5),
        'rel_bias': nrm(ks[16], (REL_BUCKETS, N_ATT_HEADS), 0.5),
    }

def first_block(x, c, ada_w, ada_b, norm_pre, norm_post, ffn_w_in, ffn_w_out, hyb_w_in, hyb_w_out,
              pool_w, pool_scale, hgrn_lb_logits, hgrn_out_norm, att_w_qkv, att_w_out, rel_bias):
    lb_cum = jnp.cumsum(jax.nn.softmax(hgrn_lb_logits.astype(jnp.float32), axis=0), axis=0)
    lower_bounds = jnp.maximum(lb_cum - lb_cum[:1], 0.0)
    split_at = [POOL_WIDTH, POOL_WIDTH + HGRN_KW, POOL_WIDTH + 2 * HGRN_KW, POOL_WIDTH + 2 * HGRN_KW + HGRN_VW]

    for layer in range(DEPTH):
        j = layer // 2
        if layer % 2 == 0:
            def mixer(h, j=j):
                u, qr, fr, vr, gr = jnp.split(h @ hyb_w_in[j], split_at, axis=-1)
                y = jnp.concatenate([pool_mixer(u, pool_w[j], pool_scale[j]),
                                     hgrn2_mixer(qr, fr, vr, gr, lower_bounds[j], hgrn_out_norm[j])], axis=-1)
                return y @ hyb_w_out[j]
        else:
            def mixer(h, j=j):
                return dilated_attention_mixer(h @ att_w_qkv[j], rel_bias) @ att_w_out[j]

        def ffn(h, l=layer):
            return swiglu(h, ffn_w_in[l], ffn_w_out[l])

        x = sandwich(x, modulation(c, ada_w[layer, 0], ada_b[layer, 0]), norm_pre[layer, 0], norm_post[layer, 0], mixer)
        x = sandwich(x, modulation(c, ada_w[layer, 1], ada_b[layer, 1]), norm_pre[layer, 1], norm_post[layer, 1], ffn)
    return x


PLE_DIM = 256
Q_BLOCK = 128
RNN_WIDTH = 512
RNN_BLOCKS = 8
CONV_WIDTH = 4
LRU_C = 8.0
DSA_HEADS = 8
DSA_HEAD_DIM = 64
IDX_HEADS = 4
IDX_DIM = 64
DSA_TOPK_MAX = 256
MLA_HEADS = 16
MLA_Q_LORA = 512
MLA_KV_LORA = 256
MLA_NOPE = 64
MLA_ROPE = 32
MLA_V = 64
ROPE_BASE = 10000.0
D_FF_2 = 4 * D_MODEL
DN_ALPHA = (2 * DEPTH) ** 0.25
DN_BETA = (8 * DEPTH) ** -0.25
LN_EPS = 1e-5
RMS_EPS = 1e-6
N_EVEN = (DEPTH + 1) // 2
N_ODD = DEPTH // 2
EVEN_SPLITS = (RNN_WIDTH, RNN_WIDTH, DSA_HEADS * DSA_HEAD_DIM, DSA_HEAD_DIM, DSA_HEAD_DIM,
               IDX_HEADS * IDX_DIM, IDX_DIM, IDX_HEADS)
EVEN_IN = sum(EVEN_SPLITS)
EVEN_MIX = RNN_WIDTH + DSA_HEADS * DSA_HEAD_DIM
MLA_DOWN = MLA_Q_LORA + MLA_KV_LORA + MLA_ROPE
MLA_MIX = MLA_HEADS * MLA_V


def layer_norm(x, g, b):
    xf = x.astype(jnp.float32)
    mu = jnp.mean(xf, axis=-1, keepdims=True)
    var = jnp.mean(jnp.square(xf - mu), axis=-1, keepdims=True)
    y = (xf - mu) * lax.rsqrt(var + LN_EPS) * g.astype(jnp.float32) + b.astype(jnp.float32)
    return y.astype(x.dtype)

def rms_norm_2(x, g):
    xf = x.astype(jnp.float32)
    y = xf * lax.rsqrt(jnp.mean(jnp.square(xf), axis=-1, keepdims=True) + RMS_EPS)
    return (y * g.astype(jnp.float32)).astype(x.dtype)

def causal_depthwise_conv(x, w, b):
    c = x.shape[-1]
    y = lax.conv_general_dilated(x, w[:, None, :], window_strides=(1,), padding=[(CONV_WIDTH - 1, 0)],
                                 dimension_numbers=("NWC", "WIO", "NWC"), feature_group_count=c)
    return y + b

def rg_lru(x, w_a, b_a, w_x, b_x, lam):
    bsz, s, c = x.shape
    xb = x.reshape(bsz, s, RNN_BLOCKS, c // RNN_BLOCKS)
    r = jax.nn.sigmoid(jnp.einsum("bsnc,ncd->bsnd", xb, w_a).reshape(bsz, s, c) + b_a)
    i = jax.nn.sigmoid(jnp.einsum("bsnc,ncd->bsnd", xb, w_x).reshape(bsz, s, c) + b_x)
    log_a = -LRU_C * r.astype(jnp.float32) * jax.nn.softplus(-lam.astype(jnp.float32))
    a = jnp.exp(log_a)
    u = jnp.sqrt(-jnp.expm1(2.0 * log_a)) * (i * x).astype(jnp.float32)

    def combine(left, right):
        a1, b1 = left
        a2, b2 = right
        return a1 * a2, a2 * b1 + b2

    _, h = lax.associative_scan(combine, (a, u), axis=1)
    return h.astype(x.dtype)

def alibi_slopes(n):
    return jnp.exp2(-8.0 * (jnp.arange(n, dtype=jnp.float32) + 1.0) / n)

def rope(x, cos, sin):
    half = x.shape[-1] // 2
    x1, x2 = x[..., :half], x[..., half:]
    return jnp.concatenate([x1 * cos - x2 * sin, x2 * cos + x1 * sin], axis=-1)

def to_blocks(a, nb):
    a = a.reshape((a.shape[0], nb, Q_BLOCK) + a.shape[2:])
    return jnp.moveaxis(a, 1, 0)

def from_blocks(o):
    o = jnp.moveaxis(o, 0, 1)
    return o.reshape((o.shape[0], o.shape[1] * o.shape[2]) + o.shape[3:])

def gather_rows(src, idx):
    return jax.vmap(lambda sb, ib: sb[ib])(src, idx)

def dsa_attention(q, k, v, iq, ik, iw):
    bsz, s = q.shape[:2]
    nb = s // Q_BLOCK
    topk = min(DSA_TOPK_MAX, s // 4)
    slopes = alibi_slopes(DSA_HEADS)
    key_pos = jnp.arange(s, dtype=jnp.int32)
    iw = iw.astype(jnp.float32) * (IDX_HEADS ** -0.5 * IDX_DIM ** -0.5)

    def block(args):
        qb, iqb, iwb, t0 = args
        qpos = t0 + jnp.arange(Q_BLOCK, dtype=jnp.int32)
        dots = jnp.einsum("bthd,bsd->bths", iqb, ik).astype(jnp.float32)
        isc = jnp.einsum("bths,bth->bts", jax.nn.relu(dots), iwb)
        causal = key_pos[None, :] <= qpos[:, None]
        isc = jnp.where(causal[None], isc, -jnp.inf)
        _, idx = lax.top_k(isc, topk)
        ksel = gather_rows(k, idx)
        vsel = gather_rows(v, idx)
        logits = jnp.einsum("bthd,btkd->bthk", qb, ksel).astype(jnp.float32) * (DSA_HEAD_DIM ** -0.5)
        dist = qpos[None, :, None] - idx
        logits = logits - slopes[None, None, :, None] * dist.astype(jnp.float32)[:, :, None, :]
        logits = jnp.where((dist >= 0)[:, :, None, :], logits, -jnp.inf)
        probs = jax.nn.softmax(logits, axis=-1).astype(v.dtype)
        return jnp.einsum("bthk,btkd->bthd", probs, vsel)

    starts = jnp.arange(nb, dtype=jnp.int32) * Q_BLOCK
    out = lax.map(block, (to_blocks(q, nb), to_blocks(iq, nb), to_blocks(iw, nb), starts))
    return from_blocks(out)

def mla_attention(q, k, v):
    bsz, s = q.shape[:2]
    nb = s // Q_BLOCK
    scale = q.shape[-1] ** -0.5
    key_pos = jnp.arange(s, dtype=jnp.int32)

    def block(args):
        qb, t0 = args
        qpos = t0 + jnp.arange(Q_BLOCK, dtype=jnp.int32)
        logits = jnp.einsum("bthd,bshd->bhts", qb, k).astype(jnp.float32) * scale
        causal = key_pos[None, :] <= qpos[:, None]
        logits = jnp.where(causal[None, None], logits, -jnp.inf)
        probs = jax.nn.softmax(logits, axis=-1).astype(v.dtype)
        return jnp.einsum("bhts,bshd->bthd", probs, v)

    starts = jnp.arange(nb, dtype=jnp.int32) * Q_BLOCK
    out = lax.map(block, (to_blocks(q, nb), starts))
    return from_blocks(out)

def hybrid_mixer(x, w_in, conv_w, conv_b, ga_w, ga_b, gx_w, gx_b, lam, w_out):
    bsz, s, _ = x.shape
    proj = x @ w_in
    split_points = np.cumsum(EVEN_SPLITS)[:-1].tolist()
    xr, yr, q, k, v, iq, ik, iw = jnp.split(proj, split_points, axis=-1)
    xr = causal_depthwise_conv(xr, conv_w, conv_b)
    rec = rg_lru(xr, ga_w, ga_b, gx_w, gx_b, lam) * jax.nn.gelu(yr)
    att = dsa_attention(q.reshape(bsz, s, DSA_HEADS, DSA_HEAD_DIM), k, v,
                        iq.reshape(bsz, s, IDX_HEADS, IDX_DIM), ik, iw)
    mixed = jnp.concatenate([rec, att.reshape(bsz, s, DSA_HEADS * DSA_HEAD_DIM)], axis=-1)
    return mixed @ w_out

def mla_mixer(x, w_down, q_norm, kv_norm, w_uq, w_ukv, w_out):
    bsz, s, _ = x.shape
    down = x @ w_down
    cq, ckv, kr = jnp.split(down, [MLA_Q_LORA, MLA_Q_LORA + MLA_KV_LORA], axis=-1)
    q = (rms_norm_2(cq, q_norm) @ w_uq).reshape(bsz, s, MLA_HEADS, MLA_NOPE + MLA_ROPE)
    kv = (rms_norm_2(ckv, kv_norm) @ w_ukv).reshape(bsz, s, MLA_HEADS, MLA_NOPE + MLA_V)
    q_nope, q_rope = q[..., :MLA_NOPE], q[..., MLA_NOPE:]
    k_nope, v = kv[..., :MLA_NOPE], kv[..., MLA_NOPE:]
    pos = jnp.arange(s, dtype=jnp.float32)
    freq = ROPE_BASE ** (-jnp.arange(0, MLA_ROPE, 2, dtype=jnp.float32) / MLA_ROPE)
    ang = pos[:, None] * freq[None, :]
    cos = jnp.cos(ang).astype(x.dtype)
    sin = jnp.sin(ang).astype(x.dtype)
    q_rope = rope(q_rope, cos[:, None, :], sin[:, None, :])
    k_rope = rope(kr, cos, sin)
    qf = jnp.concatenate([q_nope, q_rope], axis=-1)
    kf = jnp.concatenate([k_nope, jnp.broadcast_to(k_rope[:, :, None, :], (bsz, s, MLA_HEADS, MLA_ROPE))], axis=-1)
    o = mla_attention(qf, kf, v)
    return o.reshape(bsz, s, MLA_MIX) @ w_out

def second_inputs(seed: int = 0) -> dict:
    key = jax.random.key(seed)
    ks = jax.random.split(key, 32)

    def nrm(k, shape, scale):
        return jax.random.normal(k, shape, jnp.float32) * scale

    u = jax.random.uniform(ks[12], (N_EVEN, RNN_WIDTH), jnp.float32, 0.9, 0.999)
    sig = u ** (1.0 / LRU_C)
    lam = jnp.log(sig) - jnp.log1p(-sig)
    bw = RNN_WIDTH // RNN_BLOCKS
    return {
        "x": nrm(ks[0], (BATCH, SEQ, D_MODEL), 1.0),
        "p": nrm(ks[1], (DEPTH, BATCH, SEQ, PLE_DIM), 1.0),
        "ln1_g": 1.0 + nrm(ks[2], (DEPTH, D_MODEL), 0.02),
        "ln1_b": nrm(ks[3], (DEPTH, D_MODEL), 0.02),
        "ln2_g": 1.0 + nrm(ks[4], (DEPTH, D_MODEL), 0.02),
        "ln2_b": nrm(ks[5], (DEPTH, D_MODEL), 0.02),
        "mlp_w1": nrm(ks[6], (DEPTH, D_MODEL, D_FF_2), D_MODEL ** -0.5),
        "mlp_w2": nrm(ks[7], (DEPTH, D_FF_2, D_MODEL), DN_BETA * D_FF_2 ** -0.5),
        "ple_w_proj": nrm(ks[8], (DEPTH, PLE_DIM, D_MODEL), DN_BETA * PLE_DIM ** -0.5),
        "ple_w_gate": nrm(ks[9], (DEPTH, D_MODEL, D_MODEL), D_MODEL ** -0.5),
        "hy_w_in": nrm(ks[10], (N_EVEN, D_MODEL, EVEN_IN), D_MODEL ** -0.5),
        "hy_conv_w": nrm(ks[11], (N_EVEN, CONV_WIDTH, RNN_WIDTH), CONV_WIDTH ** -0.5),
        "hy_conv_b": nrm(ks[13], (N_EVEN, RNN_WIDTH), 0.01),
        "hy_ga_w": nrm(ks[14], (N_EVEN, RNN_BLOCKS, bw, bw), bw ** -0.5),
        "hy_ga_b": nrm(ks[15], (N_EVEN, RNN_WIDTH), 0.01),
        "hy_gx_w": nrm(ks[16], (N_EVEN, RNN_BLOCKS, bw, bw), bw ** -0.5),
        "hy_gx_b": nrm(ks[17], (N_EVEN, RNN_WIDTH), 0.01),
        "hy_lambda": lam,
        "hy_w_out": nrm(ks[18], (N_EVEN, EVEN_MIX, D_MODEL), DN_BETA * EVEN_MIX ** -0.5),
        "mla_w_down": nrm(ks[19], (N_ODD, D_MODEL, MLA_DOWN), D_MODEL ** -0.5),
        "mla_q_norm": 1.0 + nrm(ks[20], (N_ODD, MLA_Q_LORA), 0.02),
        "mla_kv_norm": 1.0 + nrm(ks[21], (N_ODD, MLA_KV_LORA), 0.02),
        "mla_w_uq": nrm(ks[22], (N_ODD, MLA_Q_LORA, MLA_HEADS * (MLA_NOPE + MLA_ROPE)), MLA_Q_LORA ** -0.5),
        "mla_w_ukv": nrm(ks[23], (N_ODD, MLA_KV_LORA, MLA_HEADS * (MLA_NOPE + MLA_V)), MLA_KV_LORA ** -0.5),
        "mla_w_out": nrm(ks[24], (N_ODD, MLA_MIX, D_MODEL), DN_BETA * MLA_MIX ** -0.5),
    }

def second_block(x, p, ln1_g, ln1_b, ln2_g, ln2_b, mlp_w1, mlp_w2, ple_w_proj, ple_w_gate,
              hy_w_in, hy_conv_w, hy_conv_b, hy_ga_w, hy_ga_b, hy_gx_w, hy_gx_b, hy_lambda, hy_w_out,
              mla_w_down, mla_q_norm, mla_kv_norm, mla_w_uq, mla_w_ukv, mla_w_out):
    for i in range(DEPTH):
        j = i // 2
        if i % 2 == 0:
            m = hybrid_mixer(x, hy_w_in[j], hy_conv_w[j], hy_conv_b[j], hy_ga_w[j], hy_ga_b[j],
                             hy_gx_w[j], hy_gx_b[j], hy_lambda[j], hy_w_out[j])
        else:
            m = mla_mixer(x, mla_w_down[j], mla_q_norm[j], mla_kv_norm[j], mla_w_uq[j],
                          mla_w_ukv[j], mla_w_out[j])
        h = layer_norm(DN_ALPHA * x + m, ln1_g[i], ln1_b[i])
        f = jnp.square(jax.nn.relu(h @ mlp_w1[i])) @ mlp_w2[i]
        e = jax.nn.sigmoid(h @ ple_w_gate[i]) * (p[i] @ ple_w_proj[i])
        x = layer_norm(DN_ALPHA * h + f + e, ln2_g[i], ln2_b[i])
    return x


def setup_inputs(seed=0):
    out = dict(first_inputs(seed))
    for name, value in second_inputs(seed + 1).items():
        if name != "x":
            out[name + "_2"] = value
    return out


def reference(
    x, c, ada_w, ada_b, norm_pre, norm_post, ffn_w_in, ffn_w_out, hyb_w_in, hyb_w_out, pool_w,
    pool_scale, hgrn_lb_logits, hgrn_out_norm, att_w_qkv, att_w_out, rel_bias, p_2, ln1_g_2,
    ln1_b_2, ln2_g_2, ln2_b_2, mlp_w1_2, mlp_w2_2, ple_w_proj_2, ple_w_gate_2, hy_w_in_2,
    hy_conv_w_2, hy_conv_b_2, hy_ga_w_2, hy_ga_b_2, hy_gx_w_2, hy_gx_b_2, hy_lambda_2,
    hy_w_out_2, mla_w_down_2, mla_q_norm_2, mla_kv_norm_2, mla_w_uq_2, mla_w_ukv_2, mla_w_out_2,
):
    x = first_block(
        x, c, ada_w, ada_b, norm_pre, norm_post, ffn_w_in, ffn_w_out, hyb_w_in, hyb_w_out,
        pool_w, pool_scale, hgrn_lb_logits, hgrn_out_norm, att_w_qkv, att_w_out, rel_bias,
    )
    return second_block(
        x, p_2, ln1_g_2, ln1_b_2, ln2_g_2, ln2_b_2, mlp_w1_2, mlp_w2_2, ple_w_proj_2,
        ple_w_gate_2, hy_w_in_2, hy_conv_w_2, hy_conv_b_2, hy_ga_w_2, hy_ga_b_2, hy_gx_w_2,
        hy_gx_b_2, hy_lambda_2, hy_w_out_2, mla_w_down_2, mla_q_norm_2, mla_kv_norm_2,
        mla_w_uq_2, mla_w_ukv_2, mla_w_out_2,
    )


_drawn_inputs = setup_inputs


def setup_inputs(seed=0):
    import zlib

    import numpy as np

    out = dict(_drawn_inputs(seed))
    spreads = {}
    factors = {'hy_conv_b_2': 7.761,
     'hy_ga_b_2': 8.0,
     'hy_gx_b_2': 8.0,
     'mla_q_norm_2': 8.0,
     'mla_kv_norm_2': 8.0}
    for name, (base, spread) in spreads.items():
        noise = np.random.default_rng([zlib.crc32(name.encode()), seed]).standard_normal(out[name].shape)
        drawn = base * np.exp(spread * noise) if base else spread * noise
        out[name] = __import__('jax').numpy.asarray(drawn.astype(out[name].dtype))
    for name, factor in factors.items():
        out[name] = (out[name] * factor).astype(out[name].dtype)
    return out
```

```python
from contextlib import ExitStack

import numpy as np
import concourse.bass as bass
from concourse import mybir

F32 = mybir.dt.float32
F32R = mybir.dt.float32r
ACT = mybir.ActivationFunctionType
ALU = mybir.AluOpType
AX_X = mybir.AxisListType.X

P = 128
T = 512
TT = T // P
D = 1024
DC = D // P
FF = 2816
FF_PARTS = (12, 10)
FF2_PARTS = (16, 16)
HGRN_H = 4
POOL_WINDOWS = (2, 4, 8, 16)
LEVELS = (64, 32, 16, 8, 4, 2, 1)
DIL = (1, 4, 16)
ATT_SCALE = 0.125
DSA_H, IDX_H, TOPK = 8, 4, 128
MLA_SCALE = 96.0 ** -0.5
ALPHA = 4.0 ** 0.25
EPS_RMS, EPS_LN = 1e-6, 1e-5
NEG = -1.0e30
TAKEN = -3.0e38
UNIT = 2048
BIAS_PITCH = 640


def unit_plan():
    plan = [("hyb_in", DC, 256)] * 10 + [("hyb_out", DC, 256)] * 4
    ffn = []
    for n in FF_PARTS:
        ffn += [("ffn_in", DC, 256)] * n + [("ffn_out", n, 128)] * DC
    mlp = [("gate", DC, 256)] * 4 + [("ple", 2, 512)] * 2
    for n in FF2_PARTS:
        mlp += [("mlp_in", DC, 256)] * (n // 2) + [("mlp_out", n, 128)] * DC
    plan += ffn
    for _ in range(4):
        plan += [("qkv", DC, 256)] * 4 + [("qkv", DC, 128)]
    plan += [("att_out", 4, 512)] * 2 + ffn
    plan += [("hy_in", DC, 256)] * 2 + [("hy_in", DC, 128)] + [("hy_in", DC, 256)] * 6
    plan += [("hy_out", DC, 256)] * 4 + mlp
    plan += [("mla_down", DC, 256)] * 3 + [("mla_down", DC, 128)]
    for _ in range(4):
        plan += [("mla_q", 4, 384), ("mla_kv", 2, 512)]
    plan += [("mla_out", DC, 256)] * 4 + mlp
    return plan


PLAN = unit_plan()

VEC = {}


def _vec_columns():
    at = 0
    for name, n in (("c", DC), ("ada_b", 96), ("norm_pre", 4 * DC), ("norm_post", 4 * DC), ("pool_scale", 4),
                    ("out_norm", 1), ("conv_w", 16), ("conv_b", 4), ("ga_b", 4), ("gx_b", 4), ("lam", 4),
                    ("ln1_g", 16), ("ln1_b", 16), ("ln2_g", 16), ("ln2_b", 16), ("q_norm", 4), ("kv_norm", 2), ("poolw", 4 * P),
                    ("gates", 8 * P)):
        VEC[name] = (at, n)
        at += n
    return at


NVEC = _vec_columns()

CST = {}


def _cst_columns():
    at = 0
    for name, n in (("ident", P), ("ones", P), ("perm", P), ("level", 7 * P), ("reset", T),
                    ("causal", P), ("delta", T), ("cos", T), ("sin", T), ("inv", 64)):
        CST[name] = (at, n)
        at += n
    return at


NCST = _cst_columns()



def stop_units(stop):
    u = 0
    for k in range(1, stop + 1):
        last = {1: "hyb_out", 3: "att_out", 5: "hy_out", 6: "mlp_out", 7: "mla_out", 8: "mlp_out"}.get(k, "ffn_out")
        while PLAN[u][0] != last:
            u += 1
        first = {2: FF_PARTS, 4: FF_PARTS, 6: FF2_PARTS, 8: FF2_PARTS}.get(k)
        if first:
            while u < len(PLAN) and PLAN[u][0] in (last, "ffn_in", "mlp_in"):
                u += 1
        else:
            while u < len(PLAN) and PLAN[u][0] == last:
                u += 1
    return u


def runs(plan, first):
    out, u = [], first
    while u < len(plan):
        size, k = plan[u][1] * plan[u][2], u
        while k < len(plan) and plan[k][1] * plan[k][2] == size:
            k += 1
        out.append((u, k - u, size))
        u = k
    return out


class Semaphores:
    pass


class State:
    u = tile = 0
    ev = None


class Step:

    def __init__(self, j, qks, adds, vs, w, col, last, lag, scale, nout, chunk, slope, S, PT, O, Y):
        self.j, self.qks, self.adds, self.vs, self.w, self.col, self.last = j, qks, adds, vs, w, col, last
        self.lag, self.scale, self.nout, self.chunk, self.slope = lag, scale, nout, chunk, slope
        self.S, self.PT, self.O, self.Y = S, PT, O, Y
        self.i = 0


class Counts:

    def __init__(self):
        self.v = {}

    def up(self, sem, by=1):
        e, o = self.v.get(id(sem), (0, 0))
        self.v[id(sem)] = (e, o + by)
        return e + (o + by)

    def at(self, sem):
        e, o = self.v.get(id(sem), (0, 0))
        return e + o

    def loop(self, eng, rounds, per):
        return Loop(self, eng, rounds, per)


class Loop:
    def __init__(self, counts, eng, rounds, per):
        self.c, self.eng, self.rounds, self.per = counts, eng, rounds, per

    def __enter__(self):
        self.start = {q: self.c.at(q) for q in self.per}
        self.cm = self.eng.Fori(0, self.rounds)
        i = self.cm.__enter__()
        for q, by in self.per.items():
            self.c.v[id(q)] = (i * by + self.start[q], 0)
        self.others = {k: v for k, v in self.c.v.items() if k not in [id(q) for q in self.per]}
        return i

    def __exit__(self, *e):
        if e[0] is not None:
            return self.cm.__exit__(*e)
        r = self.cm.__exit__(*e)
        for q, by in self.per.items():
            assert self.c.v[id(q)][1] == by, (q, self.c.v[id(q)][1], by)
            self.c.v[id(q)] = (0, self.start[q] + by * self.rounds)
        assert {k: v for k, v in self.c.v.items() if k not in [id(q) for q in self.per]} == self.others
        return r


def program(nc, a, out, stop):
    with ExitStack() as ctx:
        base = [(nc.sbuf_base + 63) // 64 * 64]

        def sb(name, shape, dt=F32, at=None):
            size = int(np.prod(shape[1:])) * 4
            off = base[0] if at is None else at
            if at is None:
                base[0] = (off + size + 31) // 32 * 32
            return nc.alloc_sbuf_tensor_at(name, shape, dt, offset=off)

        raw = sb("raw", [P, 2, UNIT])
        whi = sb("whi", [P, 2, UNIT], F32R)
        wlo = sb("wlo", [P, 2, UNIT], F32R)
        x = sb("x", [P, DC, T])
        h_at = base[0]
        hhi = sb("hhi", [P, DC, T], F32R)
        hlo = sb("hlo", [P, DC, T], F32R)
        ghi = sb("ghi", [P, 16, T], F32R)
        sc0 = base[0] - 16384
        glo = sb("glo", [P, 16, T], F32R)
        sc1 = base[0] - 16384
        m = sb("m", [P, DC, T])
        vecs = sb("vecs", [P, NVEC])
        cst = sb("cst", [P, NCST])
        mods = sb("mods", [P, 4, 24])
        small = sb("small", [P, 48])
        sq = sb("sq", [P, 2, T])
        tmp = sb("tmp", [P, 2, T])
        rstd = sb("rstd", [P, T])
        acc_first, acc = (q.rearrange("p (a n) -> p a n", a=2) for q in (tmp[:, 0, :], rstd[:, :]))
        assert base[0] <= nc.sbuf_usable_end, (base[0], nc.sbuf_usable_end)
        silu_c = small[:, 0:8]
        eps_rms, eps_ln = small[:, 8:9], small[:, 9:10]
        one_t = small[:, 10:11]
        spl = small[:, 12:16]
        decay = small[:, 16:20]
        mmax, rsum = small[:, 20:22], small[:, 22:24]
        rinv8 = small[:, 40:48]
        top8 = small[:, 32:40]

        def vec(name, i=0, n=1):
            at, _ = VEC[name]
            return vecs[:, at + i:at + i + n]

        def con(name, i=0, n=None):
            at, size = CST[name]
            return cst[:, at + i:at + i + (n or size)]

        ident, ones = con("ident"), con("ones")

        def hidden(c):
            return ghi[:, c, :], glo[:, c, :]

        def hin(c):
            return hhi[:, c, :], hlo[:, c, :]

        zq = sb("zq", [P, 4, T], F32, sc0)
        zg = sb("zg", [P, 4, T], F32, sc0 + 8192)
        zb = sb("zb", [P, 4, T], F32, sc1)
        zk = sb("zk", [P, 4, T], F32, sc1 + 8192)
        zv = sb("zv", [P, TT, T], F32, sc1 + 16384)
        zu = sb("zu", [P, 4, T], F32, sc1 + 24576)
        ze = sb("ze", [P, 2, T], F32, h_at)
        zqe = sb("zqe", [P, 2, T], F32, h_at + 4096)
        zke = sb("zke", [P, 2, T], F32, h_at + 8192)
        za = sb("za", [P, TT, P], F32, h_at + 12288)
        zkt = sb("zkt", [P, TT, P], F32, h_at + 14336)
        zs = sb("zs", [P, 3, P], F32, h_at + 16384)
        zw = sb("zw", [P, 2, T], F32, h_at + 17920)
        zt = sb("zt", [P, TT, P], F32, h_at + 22016)
        g0_at = sc0 - 16384
        onehot = sb("onehot", [P, 3 * BIAS_PITCH], F32, g0_at)
        relb = sb("relb", [P, 24], F32, g0_at + 7680)
        biasr = sb("biasr", [P, 3, BIAS_PITCH], F32, g0_at + 7808)
        qk = sb("qk", [P, 8, T], F32, sc0)
        vt = sb("vt", [P, 3, TT, P], F32, sc1)
        toep = sb("toep", [P, 6, T], F32, sc1 + 6144)
        sc = sb("sc", [P, 2, 1280], F32, sc1 + 18432)
        yt = sb("yt", [P, 1, T], F32, sc1 + 28672)
        ptd = (sb("ptd0", [P, 10, P], F32, g0_at + 8192), sb("ptd1", [P, 10, P], F32, sc1 - 8192))
        osb = sb("osb", [P, 4 * P], F32, sc1 + 30720)
        vi = sb("vi", [P, TT, P], F32, sc1)
        msk = sb("msk", [P, 1280], F32, sc1 + 2048)
        bh = sb("bh", [P, T], F32, sc1 + 7168)
        sc5 = sb("sc5", [P, 2, T], F32, sc1 + 9216)
        pt5 = (sb("pt50", [P, 4, P], F32, sc1 + 13312), sb("pt51", [P, 4, P], F32, sc1 + 25600))
        os5 = sb("os5", [P, 4 * P], F32, sc1 + 15360)
        yt5 = sb("yt5", [P, 4, T], F32, sc1 + 17408)
        xr = sb("xr", [P, 4, T], F32, sc1 + 17408)
        yr = sb("yr", [P, 4, T], F32, sc1 + 9216)
        rg = sb("rg", [P, 8, T], F32, h_at)
        krr, qrr = m[:, 6, :], m[:, 7, :]
        vm = sb("vm", [P, TT, 256], F32, sc1)
        sc7 = sb("sc7", [P, 2, T], F32, sc1 + 4096)
        pt7 = (sb("pt70", [P, 4, P], F32, sc1 + 8192), sb("pt71", [P, 4, P], F32, sc1 + 16384))
        os7 = sb("os7", [P, 4 * P], F32, sc1 + 10240)
        yt7 = sb("yt7", [P, 2, T], F32, sc1 + 12288)
        pin = sb("pin", [P, 2, T], F32, sc1)
        adw_a = [sb(f"adw_a{i}", [P, UNIT], F32, (sc0, sc0 + 8192, sc1, sc1 + 8192, sc1 + 16384, sc1 + 24576)[i])
                 for i in range(6)]
        adw_b = [sb(f"adw_b{i}", [P, UNIT], F32, (g0_at, g0_at + 8192, sc1 - 16384, sc1 - 8192)[i])
                 for i in range(4)]
        adw_c = [adw_a[1], adw_a[3]]

        s = Semaphores()
        s.vecs_in = ctx.enter_context(nc.semaphore("vecs_in"))
        s.cst_in = ctx.enter_context(nc.semaphore("cst_in"))
        s.x_in = ctx.enter_context(nc.semaphore("x_in"))
        s.raw0 = ctx.enter_context(nc.semaphore("raw0"))
        s.raw1 = ctx.enter_context(nc.semaphore("raw1"))
        s.whi_ok = ctx.enter_context(nc.semaphore("whi_ok"))
        s.wlo_ok = ctx.enter_context(nc.semaphore("wlo_ok"))
        s.ready = ctx.enter_context(nc.semaphore("ready"))
        s.mm = ctx.enter_context(nc.semaphore("mm"))
        s.ev_a = ctx.enter_context(nc.semaphore("ev_a"))
        s.ev_d = ctx.enter_context(nc.semaphore("ev_d"))
        s.silu_ok = ctx.enter_context(nc.semaphore("silu_ok"))
        s.ada_mm = ctx.enter_context(nc.semaphore("ada_mm"))
        s.sq_ok = ctx.enter_context(nc.semaphore("sq_ok"))
        s.ss_mm = ctx.enter_context(nc.semaphore("ss_mm"))
        s.rms_ok = ctx.enter_context(nc.semaphore("rms_ok"))
        s.h_ok = ctx.enter_context(nc.semaphore("h_ok"))
        s.y_ok = ctx.enter_context(nc.semaphore("y_ok"))
        s.sa_ok = ctx.enter_context(nc.semaphore("sa_ok"))
        s.x_ok = ctx.enter_context(nc.semaphore("x_ok"))
        s.dv = ctx.enter_context(nc.semaphore("dv"))
        s.av = ctx.enter_context(nc.semaphore("av"))
        s.pl = ctx.enter_context(nc.semaphore("pl"))
        s.out_ok = ctx.enter_context(nc.semaphore("out_ok"))
        s.pe_to_act = ctx.enter_context(nc.semaphore("pe_to_act"))
        s.pe_to_dve = ctx.enter_context(nc.semaphore("pe_to_dve"))
        s.act_to_pe = ctx.enter_context(nc.semaphore("act_to_pe"))
        s.act_to_dve = ctx.enter_context(nc.semaphore("act_to_dve"))
        s.dve_to_pe = ctx.enter_context(nc.semaphore("dve_to_pe"))
        s.dve_to_act = ctx.enter_context(nc.semaphore("dve_to_act"))
        s.extra_in = ctx.enter_context(nc.semaphore("extra_in"))
        s.bias_mm = ctx.enter_context(nc.semaphore("bias_mm"))
        s.bias_ok = ctx.enter_context(nc.semaphore("bias_ok"))
        s.scr_out = ctx.enter_context(nc.semaphore("scr_out"))
        s.toep_in = ctx.enter_context(nc.semaphore("toep_in"))
        s.sc_mm = ctx.enter_context(nc.semaphore("sc_mm"))
        s.sc_rd = ctx.enter_context(nc.semaphore("sc_rd"))
        s.mx_ok = ctx.enter_context(nc.semaphore("mx_ok"))
        s.pr_ok = ctx.enter_context(nc.semaphore("pr_ok"))
        s.tr_mm = ctx.enter_context(nc.semaphore("tr_mm"))
        s.pt_a = ctx.enter_context(nc.semaphore("pt_a"))
        s.pt_d = ctx.enter_context(nc.semaphore("pt_d"))
        s.pv_mm = ctx.enter_context(nc.semaphore("pv_mm"))
        s.o_ok = ctx.enter_context(nc.semaphore("o_ok"))
        s.ot_mm = ctx.enter_context(nc.semaphore("ot_mm"))
        s.yt_ok = ctx.enter_context(nc.semaphore("yt_ok"))
        s.sa_free = ctx.enter_context(nc.semaphore("sa_free"))
        s.p_in = ctx.enter_context(nc.semaphore("p_in"))
        s.p_ok = ctx.enter_context(nc.semaphore("p_ok"))
        s.rl_ok = ctx.enter_context(nc.semaphore("rl_ok"))
        s.top_ok = ctx.enter_context(nc.semaphore("top_ok"))
        s.ada_acc = ctx.enter_context(nc.semaphore("ada_acc"))
        s.nb_ok = ctx.enter_context(nc.semaphore("nb_ok"))
        s.hi_ok = ctx.enter_context(nc.semaphore("hi_ok"))
        ada_b_in = [ctx.enter_context(nc.semaphore(f"ada_b_in{i}")) for i in range(4)]
        ada_in = [ctx.enter_context(nc.semaphore(f"ada_in{i}")) for i in range(6)]
        s_raw = (s.raw0, s.raw1)
        LB = [ctx.enter_context(nc.psum_tensor(f"lin{i}", [P, T], F32)) for i in range(4)]
        B4, B5, B6, B7 = (ctx.enter_context(nc.psum_tensor(f"bank{i}", [P, T], F32)) for i in range(4, 8))

        scratch = nc.dram_tensor("bias_rows", (3, 8, P, BIAS_PITCH), F32, kind="Internal")

        def heads_pair(hp):
            steps = []
            for j in range(TT):
                for hh in range(2):
                    rows, w = slice(64 * hh, 64 * hh + 64), P * (j + 1)
                    lo = P * max(0, j - 1)
                    seg = [(0, lo, w), (1, 0, w), (2, 0, w)]
                    at, qks, adds, vs = 0, [], [], []
                    for g, k0, k1 in seg:
                        qks.append((LB[g], k1 - k0, [(qk[rows, g, j * P:(j + 1) * P], qk[rows, 3 + g, k0:k1])]))
                        adds.append((LB[g], at, k1 - k0, toep[:, 3 * hh + g, 384 - P * j + k0:384 - P * j + k1], None))
                        vs += [vt[:, g, b, 64 * hh:64 * hh + 64] for b in range(k0 // P, k1 // P)]
                        at += k1 - k0
                    steps.append(Step(j=j, qks=qks, adds=adds, vs=vs, w=at, col=64 * hh, last=hh == 1,
                                                 lag=1, scale=ATT_SCALE, nout=1, chunk=hp, slope=None,
                                                 S=sc, PT=ptd, O=osb, Y=yt))
            return steps

        def sparse_steps():
            steps = []
            for j in range(TT):
                w, moff = P * (j + 1), P * (0, 0, 2, 5)[j]
                for h in range(DSA_H):
                    rows, i = slice(64 * (h % 2), 64 * (h % 2) + 64), len(steps)
                    mask = con("causal") if j == 0 else msk[:, moff:moff + w]
                    steps.append(Step(
                        j=j, qks=[(LB[i % 2], w, [(qk[rows, 4 + h // 2, j * P:(j + 1) * P], qk[rows, 3, 0:w])])],
                        adds=[(LB[i % 2], 0, w, bh[:, 0:w], None)], vs=[vi[:, b, 0:64] for b in range(j + 1)], w=w,
                        col=64 * h, last=h == DSA_H - 1, lag=2, scale=ATT_SCALE, nout=4, chunk=4,
                        slope=(2.0 ** -(h + 1), con("delta", 384 - P * j, w), mask), S=sc5, PT=pt5, O=os5, Y=yt5))
            return steps

        def mla_steps(g):
            steps = []
            for j in range(TT):
                for h in range(4):
                    w, tj, i = P * (j + 1), slice(j * P, (j + 1) * P), len(steps)
                    steps.append(Step(
                        j=j, qks=[(LB[i % 2], w, [(qk[0:96, h, tj], qk[0:96, 4 + h, 0:w])])],
                        adds=[(LB[i % 2], j * P, P, con("causal"), None)] + ([(LB[i % 2], 0, j * P, None, None)] if j else []),
                        vs=[vm[:, b, 64 * h:64 * h + 64] for b in range(j + 1)], w=w, col=64 * h, last=h == 3, lag=2,
                        scale=MLA_SCALE, nout=2, chunk=2 * g, slope=None, S=sc7, PT=pt7, O=os7, Y=yt7))
            return steps

        block = ctx.enter_context(nc.Block())
        plan = PLAN[:stop_units(stop)]
        offs = [0]
        for _, kc, nc_ in PLAN:
            offs.append(offs[-1] + P * kc * nc_)

        def ada_unit(k):
            return a["ada"][bass.ds(k * (P * UNIT), P * UNIT)].rearrange("(p n) -> p n", p=P)

        @block.sync
        def _(sp):
            n = Counts()

            def load(dst, src, which):
                sp.dma_start(dst, src).then_inc(which, 16)

            load(vecs[:, :], a["vecs"], s.vecs_in)
            load(cst[:, :], a["cst"], s.cst_in)
            load(x[:, :, :], a["x"], s.x_in)
            for j in range(6):
                load(adw_a[j][:, :], ada_unit(j), ada_in[j])

            def unit(slot, off, size):
                load(raw[:, slot, 0:size], a["w"][bass.ds(off, P * size)].rearrange("(p n) -> p n", p=P), s_raw[slot])

            for u in range(2):
                unit(u, offs[u], plan[u][1] * plan[u][2])
            for j in range(6, 12):
                sp.wait_ge(s.ada_acc, n.up(s.ada_acc))
                load(adw_a[j - 6][:, :], ada_unit(j), ada_in[j - 6])
            for j in range(4):
                load(adw_b[j][:, :], ada_unit(12 + j), ada_b_in[j])
            for u0, count, size in runs(plan, 2):
                pairs = count // 2 if count >= 4 else 0
                if pairs:
                    with n.loop(sp, pairs, {s.wlo_ok: 2}) as i:
                        for j in range(2):
                            sp.wait_ge(s.wlo_ok, n.up(s.wlo_ok))
                            unit((u0 + j) % 2, i * (2 * P * size) + (offs[u0] + j * P * size), size)
                for u in range(u0 + 2 * pairs, u0 + count):
                    sp.wait_ge(s.wlo_ok, n.up(s.wlo_ok))
                    unit(u % 2, offs[u], size)
            sp.wait_ge(s.x_ok, 8 * stop)
            sp.dma_start(out, x[:, :, :]).then_inc(s.out_ok, 16)
            sp.wait_ge(s.out_ok, 16)

        @block.gpsimd
        def _(pool):
            n = Counts()
            nc.gpsimd.memset(small[:, 8:9], EPS_RMS).then_inc(s.pl, 1)
            nc.gpsimd.memset(small[:, 9:10], EPS_LN).then_inc(s.pl, 1)
            nc.gpsimd.memset(small[:, 10:11], 1.0).then_inc(s.pl, 1)
            pool.wait_ge(s.pl, 3)
            nc.gpsimd.memset(small[:, 11:12], 0.0).then_inc(s.ready, 1)

            def low(slot, size):
                pool.wait_ge(s.whi_ok, n.up(s.whi_ok))
                nc.gpsimd.tensor_tensor(wlo[:, slot, 0:size], raw[:, slot, 0:size],
                                        whi[:, slot, 0:size].bitcast(F32), ALU.subtract).then_inc(s.wlo_ok, 1)

            for u0, count, size in runs(plan, 0):
                pairs = count // 2 if count >= 4 else 0
                if pairs:
                    with n.loop(pool, pairs, {s.whi_ok: 2}):
                        for j in range(2):
                            low((u0 + j) % 2, size)
                for u in range(u0 + 2 * pairs, u0 + count):
                    low(u % 2, size)

        @block.tensor
        def _(pe):
            n = Counts()
            st = State()

            def switch(ev):
                if st.ev is not None and st.ev is not ev:
                    pe.wait_ge(st.ev, n.at(st.ev) + 4)
                st.ev = ev

            def bank_free():
                pe.wait_ge(st.ev, n.up(st.ev))

            def three(dst, lh, ll, rh, rl, first, last):
                pe.matmul(dst, lh, rh, start=first, stop=False)
                pe.matmul(dst, lh, rl, start=False, stop=False)
                return pe.matmul(dst, ll, rh, start=False, stop=last)

            def fm_unit(slot, tile0, kc, tiles, xs, chunks=None, after=None, wid=None):
                pe.wait_ge(s.wlo_ok, n.up(s.wlo_ok))
                w = wid or tiles * P
                for t in range(tiles):
                    bank_free()
                    dst = LB[(tile0 + t) % 4]
                    for c in range(kc):
                        if chunks is not None and t == 0:
                            pe.wait_ge(chunks[0], chunks[1] + c + 1)
                        at = c * w + t * P
                        hi, lo = xs(c)
                        mm = three(dst[:, :], whi[:, slot, at:at + P], wlo[:, slot, at:at + P], hi, lo,
                                   c == 0, c == kc - 1)
                    mm.then_inc(s.mm, 1)
                    if after is not None:
                        after(t)

            def tok_unit(slot, tile0, kc, wid, col0, cols, xs):
                for t in range(TT):
                    bank_free()
                    dst = LB[(tile0 + t) % 4]
                    for c in range(kc):
                        at = c * wid + col0
                        hi, lo = xs(c)
                        tk = slice(t * P, (t + 1) * P)
                        mm = three(dst[:, 0:cols], hi[:, tk], lo[:, tk], whi[:, slot, at:at + cols],
                                   wlo[:, slot, at:at + cols], c == 0, c == kc - 1)
                    mm.then_inc(s.mm, 1)

            def lin(units, xs, chunks=None, after=None):
                _, kc, w = plan[st.u]
                first = None if chunks is None else (chunks, n.at(chunks))
                for j in range(units):
                    fm_unit(st.u % 2, st.tile, kc, w // P, xs, first if j == 0 else None,
                            None if after is None else (lambda t, j=j: after(j * (w // P) + t)))
                    st.u += 1
                    st.tile += w // P
                if chunks is not None:
                    n.up(chunks, kc)

            def lin_loop(units, xs, chunks=None, after=None):
                _, kc, w = plan[st.u]
                step = 4 * P // w
                assert units % step == 0 and step % 2 == 0
                first = None if chunks is None else (chunks, n.at(chunks))
                moved = {s.wlo_ok: step, st.ev: 4}
                if after is not None:
                    moved[s.ada_acc] = 2
                with n.loop(pe, units // step, moved) as i:
                    for j in range(step):
                        fm_unit((st.u + j) % 2, st.tile + j * (w // P), kc, w // P, xs, first if j == 0 else None,
                                None if after is None else (lambda t, j=j: after(i, j * (w // P) + t)))
                st.u += units
                st.tile += units * (w // P)
                if chunks is not None:
                    n.up(chunks, kc)

            def feature_sum(k, last=DC - 1, dst=None):
                pe.wait_ge(s.sq_ok, n.up(s.sq_ok))
                pe.matmul(B4[:, :], ones, sq[:, k % 2, :], start=(k == 0), stop=(k == last)).then_inc(s.ss_mm, 1)

            def norm_sums():
                for c in range(DC):
                    feature_sum(c)

            def sums_after(t):
                if t >= 1:
                    feature_sum(t - 1)
                if t == DC - 1:
                    feature_sum(t)

            def ada_sum(k, col, acc=acc):
                pe.wait_ge(s.ada_acc, n.up(s.ada_acc))
                for f in range(2):
                    mm = pe.matmul(B5[:, bass.ds(col + f, 1)], acc[:, k % 2, f * P:f * P + P], ones[:, 0:1],
                                   start=True, stop=True)
                mm.then_inc(s.ada_mm, 1)

            def hgrn_mixer():
                switch(s.ev_a)
                lin(6, hin, s.h_ok, lambda t: ada_sum(t, 2 * t))
                for _ in range(2):
                    pe.wait_ge(s.wlo_ok, n.up(s.wlo_ok))
                    tok_unit(st.u % 2, st.tile, DC, 256, 0, 256, hin)
                    st.u, st.tile = st.u + 1, st.tile + 4
                lin(2, hin)
                for g in range(4):
                    pe.wait_ge(s.dve_to_pe, n.up(s.dve_to_pe))
                    pe.matmul((B4, B5)[g % 2][:, :], vec("poolw", g * P, P), zw[:, g % 2, :], start=True, stop=True)\
                        .then_inc(s.pe_to_dve, 1)
                for h in range(HGRN_H):
                    for l in range(len(LEVELS) + 1):
                        pe.wait_ge(s.dve_to_pe, n.up(s.dve_to_pe))
                        q_, k_ = (zqe[:, l % 2, :], zke[:, l % 2, :]) if l < len(LEVELS) else (zq[:, h, :], zk[:, h, :])
                        for t in range(TT):
                            tk = slice(t * P, (t + 1) * P)
                            mm = pe.matmul((B4, B5)[l % 2][:, tk], k_[:, tk], q_[:, tk], start=True, stop=True)
                        mm.then_inc(s.pe_to_dve, 1)
                    pe.wait_ge(s.dve_to_pe, n.up(s.dve_to_pe))
                    for t in range(TT):
                        tk = slice(t * P, (t + 1) * P)
                        mm = pe.transpose(B7[:, tk], zke[:, 0, tk], ident)
                    mm.then_inc(s.pe_to_act, 1)
                    pe.wait_ge(s.act_to_pe, n.up(s.act_to_pe))
                    hv = slice(h * P, (h + 1) * P)
                    for t in range(TT - 1):
                        mm = pe.matmul(B7[:, t * P:(t + 1) * P], zkt[:, t, :], zv[:, t, hv], start=True, stop=True)
                    mm.then_inc(s.pe_to_dve, 1)
                    for t in range(TT):
                        tk = slice(t * P, (t + 1) * P)
                        if t == 1:
                            pe.wait_ge(s.dve_to_pe, n.up(s.dve_to_pe))
                        mm = pe.matmul(B6[:, tk], zv[:, t, hv], za[:, t, :], start=True, stop=(t == 0))
                        if t:
                            mm = pe.matmul(B6[:, tk], zs[:, t - 1, :], zqe[:, 1, tk], start=False, stop=True)
                    mm.then_inc(s.pe_to_act, 1)
                    pe.wait_ge(s.act_to_pe, n.up(s.act_to_pe))
                    pe.matmul(B4[:, :], ones, sq[:, 0, :], start=True, stop=True).then_inc(s.pe_to_act, 1)
                switch(s.ev_a)
                lin(4, hidden, s.y_ok, sums_after)

            def bias_rows():
                pe.wait_ge(st.ev, n.at(st.ev) + 4)
                pe.wait_ge(s.extra_in, 32)
                for g in range(3):
                    for k in range(2):
                        at = g * BIAS_PITCH + k * 320
                        pe.matmul((LB + [B6, B7])[2 * g + k][0:8, 0:320], relb[0:33, 8 * g:8 * g + 8],
                                  onehot[0:33, at:at + 320], start=True, stop=True).then_inc(s.bias_mm, 1)
                pe.wait_ge(s.bias_ok, 6)

            def attention(steps):
                base = n.at(s.sc_rd)
                turn = []

                def turn_out():
                    while turn:
                        q = turn.pop()
                        pe.wait_ge(s.o_ok, n.up(s.o_ok))
                        if q.i > len(steps) // TT:
                            pe.wait_ge(s.yt_ok, n.up(s.yt_ok))
                        for k in range(q.nout):
                            mm = pe.transpose(LB[3][:, k * P:(k + 1) * P], q.O[:, k * P:(k + 1) * P], ident)
                        mm.then_inc(s.ot_mm, 1)

                for i in range(len(steps) + 4):
                    if i < len(steps):
                        q = steps[i]
                        q.i = i
                        if i >= q.lag:
                            pe.wait_ge(s.sc_rd, base + i - q.lag + 1)
                        for bank, w, parts in q.qks:
                            for k, (lh, rh) in enumerate(parts):
                                mm = pe.matmul(bank[:, 0:w], lh, rh, start=(k == 0), stop=(k == len(parts) - 1))
                        mm.then_inc(s.sc_mm, 1)
                    turn_out()
                    if 2 <= i < len(steps) + 2:
                        q = steps[i - 2]
                        nb = q.w // P
                        pe.wait_ge(s.pt_a, n.up(s.pt_a))
                        pe.wait_ge(s.pt_d, n.up(s.pt_d))
                        for b in range(nb):
                            mm = pe.matmul(B7[:, q.col:q.col + 64], q.PT[i % 2][:, b, :], q.vs[b],
                                           start=(b == 0), stop=(b == nb - 1))
                        if q.last:
                            mm.then_inc(s.pv_mm, 1)
                            turn.append(q)
                    if 1 <= i <= len(steps):
                        q = steps[i - 1]
                        pe.wait_ge(s.pr_ok, n.up(s.pr_ok))
                        for b in range(q.w // P):
                            mm = pe.transpose((B4, B5, B6)[b // 4][:, (b % 4) * P:(b % 4 + 1) * P],
                                              q.S[:, (i - 1) % 2, b * P:(b + 1) * P], ident)
                        mm.then_inc(s.tr_mm, 1)
                n.up(s.sc_rd, len(steps))
                pe.wait_ge(s.sc_rd, n.at(s.sc_rd))
                pe.wait_ge(s.yt_ok, n.up(s.yt_ok))

            def project_in():
                pe.wait_ge(st.ev, n.at(st.ev) + 4)

            def dilated_mixer():
                switch(s.ev_a)
                for hp in range(4):
                    lin(3, hin, s.h_ok if hp == 0 else None)
                    for cols in (256, 128):
                        pe.wait_ge(s.wlo_ok, n.up(s.wlo_ok))
                        tok_unit(st.u % 2, st.tile, DC, cols, 0, cols, hin)
                        st.u, st.tile = st.u + 1, st.tile + 4
                    project_in()
                    attention(heads_pair(hp))
                lin(2, hidden, s.y_ok, sums_after)

            def layer_sums(t):
                for k in ([t - 1] if t else []) + ([t] if t == DC - 1 else []):
                    pe.wait_ge(s.sq_ok, n.up(s.sq_ok))
                    pe.matmul(B5[:, :], ones, m[:, k, :], start=(k == 0), stop=(k == DC - 1))
                    pe.matmul(B4[:, :], ones, sq[:, k % 2, :], start=(k == 0), stop=(k == DC - 1)).then_inc(s.ss_mm, 1)

            def sparse_mixer():
                switch(s.ev_a)
                lin(2, hin, s.h_ok)
                pe.wait_ge(s.wlo_ok, n.up(s.wlo_ok))
                tok_unit(st.u % 2, st.tile, DC, 128, 0, 128, hin)
                st.u, st.tile = st.u + 1, st.tile + 4
                project_in()
                for j in range(1, TT):
                    for h in range(IDX_H):
                        k = (j - 1) * IDX_H + h
                        rows = slice(64 * (h % 2), 64 * (h % 2) + 64)
                        if k >= 2:
                            pe.wait_ge(s.rl_ok, n.up(s.rl_ok))
                        pe.matmul((B4, B5)[k % 2][:, 0:P * (j + 1)], qk[rows, h // 2, j * P:(j + 1) * P],
                                  qk[rows, 2, 0:P * (j + 1)], start=True, stop=True).then_inc(s.pe_to_act, 1)
                pe.wait_ge(s.rl_ok, n.up(s.rl_ok, 2))
                lin(6, hin)
                project_in()
                for t in range(4):
                    pe.wait_ge(s.dve_to_pe, n.up(s.dve_to_pe))
                    for k in range(2):
                        mm = pe.matmul((B4, B5)[k][:, :], vec("gates", (4 * k + t) * P, P), rg[:, 0, :],
                                       start=True, stop=True)
                    mm.then_inc(s.pe_to_act, 1)
                pe.wait_ge(s.top_ok, 1)
                attention(sparse_steps())
                switch(s.ev_d)
                lin(4, hidden, s.y_ok, layer_sums)

            def mla_mixer():
                switch(s.ev_a)
                lin(3, hin, s.h_ok)
                lin(1, hin)
                for c in range(6):
                    pe.wait_ge(s.sq_ok, n.up(s.sq_ok))
                    pe.matmul((B4 if c < 4 else B5)[:, :], ones, sq[:, c % 2, :], start=(c in (0, 4)),
                              stop=(c in (3, 5))).then_inc(s.ss_mm, 1)
                pe.matmul(B6[:, :], con("perm"), krr, start=True, stop=True).then_inc(s.pe_to_dve, 1)
                hb = n.at(s.h_ok)
                for g in range(4):
                    fm_unit(st.u % 2, st.tile, 4, 3, hin, (s.h_ok, hb))
                    st.u, st.tile = st.u + 1, st.tile + 3
                    if g == 0:
                        pe.wait_ge(s.h_ok, hb + 6)
                        n.up(s.h_ok, 6)
                    fm_unit(st.u % 2, st.tile, 2, 2, lambda c: hin(4 + c), None, None, 512)
                    tok_unit(st.u % 2, st.tile + 2, 2, 512, 256, 256, lambda c: hin(4 + c))
                    st.u, st.tile = st.u + 1, st.tile + 6
                    project_in()
                    if g == 0:
                        pe.wait_ge(s.dve_to_pe, n.up(s.dve_to_pe))
                    pe.matmul(B6[:, :], con("perm"), qrr, start=True, stop=True).then_inc(s.pe_to_dve, 1)
                    pe.wait_ge(s.dve_to_pe, n.up(s.dve_to_pe))
                    attention(mla_steps(g))
                switch(s.ev_d)
                lin(4, hidden, s.y_ok, layer_sums)

            def mlp():
                switch(s.ev_a)
                lin_loop(4, hin, s.h_ok)
                switch(s.ev_d)
                lin(2, lambda c: hidden(14 + c), s.p_ok)
                for part in range(2):
                    switch(s.ev_a)
                    lin_loop(8, hin)
                    switch(s.ev_d)
                    if part == 0:
                        lin_loop(8, hidden, s.y_ok)
                    else:
                        lin(8, hidden, s.y_ok, layer_sums)

            def ffn(sums=None):
                switch(s.ev_d)
                lin_loop(FF_PARTS[0], hin, s.h_ok, sums and sums(0))
                switch(s.ev_a)
                lin_loop(8, hidden, s.y_ok)
                if sums:
                    for k in range(2):
                        ada_sum(k, 24 + 2 * k)
                switch(s.ev_d)
                lin_loop(FF_PARTS[1], hin, None, sums and sums(28))
                lin(8, hidden, s.y_ok, sums_after)

            pe.wait_ge(s.ready, 1)
            pe.wait_ge(s.vecs_in, 16)
            pe.wait_ge(s.cst_in, 16)
            for k in range(12):
                ada_sum(k, 2 * k, acc_first)
            norm_sums()
            hgrn_mixer()
            if stop > 1:
                norm_sums()
                ffn(lambda col: lambda i, t: None if t % 2 else ada_sum(t // 2, i * 4 + (col + t)))
            if stop > 2:
                norm_sums()
                bias_rows()
                dilated_mixer()
            if stop > 3:
                norm_sums()
                ffn()
            if stop > 4:
                sparse_mixer()
            if stop > 5:
                mlp()
            if stop > 6:
                mla_mixer()
            if stop > 7:
                mlp()

        @block.scalar
        def _(act):
            n = Counts()
            st = State()

            def split(slot, size):
                act.wait_ge(s_raw[slot], n.up(s_raw[slot], 16))
                act.activation(whi[:, slot, 0:size], raw[:, slot, 0:size], ACT.Copy).then_inc(s.whi_ok, 1)

            def split_next():
                u = st.u + 2
                st.u += 1
                if u < len(plan):
                    split(u % 2, plan[u][1] * plan[u][2])

            tile = [0]

            def read(units, per, func, dst, width=T, after=None):
                t0 = tile[0]
                for j in range(units):
                    for t in range(per):
                        k = j * per + t
                        act.wait_ge(s.mm, n.up(s.mm))
                        if t == per - 1:
                            split_next()
                        act.activation(dst(k), LB[(t0 + k) % 4][:, 0:width], func).then_inc(s.ev_a, 1)
                        n.up(s.ev_a)
                        if after is not None:
                            after(k)
                tile[0] += units * per

            def squares(src, ready=None):
                for c in range(DC):
                    if ready is not None:
                        act.wait_ge(ready, n.up(ready))
                    if c >= 2:
                        act.wait_ge(s.ss_mm, n.up(s.ss_mm))
                    act.activation(sq[:, c % 2, :], src(c), ACT.Square).then_inc(s.sq_ok, 1)
                act.wait_ge(s.ss_mm, n.up(s.ss_mm, 2))

            def root(scale, eps):
                act.activation(rstd[:, :], B4[:, :], ACT.Sqrt, bias=eps, scale=scale).then_inc(s.rms_ok, 1)

            def pre_norm(ls, ready=s.x_ok):
                squares(lambda c: x[:, c, :], ready)
                root(1.0 / D, eps_rms)
                for c in range(DC):
                    act.wait_ge(s.nb_ok, n.up(s.nb_ok))
                    act.activation(hhi[:, c, :], tmp[:, c % 2, :], ACT.Identity, bias=mods[:, ls, c:c + 1])\
                        .then_inc(s.hi_ok, 1)

            def out_tiles(units, per, src=None):
                t0 = tile[0]
                for k in range(DC):
                    act.wait_ge(s.mm, n.up(s.mm))
                    if k % per == per - 1:
                        split_next()
                    if k >= 2:
                        act.wait_ge(s.ss_mm, n.up(s.ss_mm))
                    b = LB[(t0 + k) % 4]
                    act.activation(sq[:, k % 2, :], b[:, :], ACT.Square).then_inc(s.sq_ok, 1)
                    act.activation(m[:, k, :], b[:, :], ACT.Copy).then_inc(s.ev_a, 1)
                    n.up(s.ev_a)
                act.wait_ge(s.ss_mm, n.up(s.ss_mm, 2))
                tile[0] += DC

            def load_ada(j, k):
                act.wait_ge(s.ada_acc, n.up(s.ada_acc))
                act.dma_start(adw_c[j][:, :], ada_unit(k)).then_inc(ada_in[j], 16)

            def swiglu_in(size, ada=None):
                t0 = tile[0]
                rounds = size // 2 - 1
                moved = {s.mm: 4, s.ev_d: 4, s_raw[0]: 16, s_raw[1]: 16}
                if ada is not None:
                    moved[s.ada_acc] = 2
                with n.loop(act, rounds, moved) as i:
                    for j in range(2):
                        silu_pair(t0, j)
                        split((st.u + j) % 2, UNIT)
                        if ada is not None:
                            load_ada(j, i * 2 + (ada + 2 + j))
                st.u += 2 * rounds
                for j in range(2):
                    silu_pair(t0, j)
                    split_next()
                    if ada == 24:
                        load_ada(j, 36 + j)
                tile[0] += 2 * size

            def silu_pair(t0, j):
                act.wait_ge(s.mm, n.up(s.mm))
                act.wait_ge(s.ev_d, n.up(s.ev_d, 2))
                act.activation(tmp[:, j, :], LB[(t0 + 2 * j) % 4][:, :], ACT.Silu).then_inc(s.sa_ok, 1)
                act.wait_ge(s.mm, n.up(s.mm))

            def hgrn_mixer():
                def load_ada(j):
                    act.wait_ge(s.ada_acc, 12 + j + 1)
                    act.dma_start(adw_b[j % 4][:, :], ada_unit(16 + j)).then_inc(ada_b_in[j % 4], 16)

                read(2, 2, ACT.Silu, lambda k: zq[:, k, :], after=load_ada)
                read(2, 2, ACT.Silu, lambda k: zg[:, k, :], after=lambda k: load_ada(4 + k))
                read(2, 2, ACT.Copy, lambda k: zk[:, k, :])
                for h in range(HGRN_H):
                    act.wait_ge(s.ev_a, n.at(s.ev_a) + 4)
                    if h >= 2:
                        act.wait_ge(s.dve_to_act, n.up(s.dve_to_act))
                    act.activation(tmp[:, h % 2, :], zk[:, h, :], ACT.Abs).then_inc(s.av, 1)
                    act.wait_ge(s.av, n.up(s.av))
                    act.activation(tmp[:, h % 2, :], tmp[:, h % 2, :], ACT.Exp, scale=-1.0).then_inc(s.av, 1)
                    act.wait_ge(s.av, n.up(s.av))
                    act.activation(tmp[:, h % 2, :], tmp[:, h % 2, :], ACT.Ln, bias=one_t).then_inc(s.act_to_dve, 1)
                act.wait_ge(s.dve_to_act, n.up(s.dve_to_act, 2))
                for h in range(HGRN_H):
                    act.activation(zk[:, h, :], zk[:, h, :], ACT.Exp).then_inc(s.act_to_dve, 1)
                for half in range(2):
                    read(1, 4, ACT.Copy, lambda k, half=half: zv[:, k, half * 256:half * 256 + 256], 256)
                read(2, 2, ACT.Copy, lambda k: zu[:, k, :])
                for h in range(HGRN_H):
                    for l in range(len(LEVELS) + 2):
                        act.wait_ge(s.dve_to_act, n.up(s.dve_to_act))
                        act.activation(ze[:, l % 2, :], ze[:, l % 2, :], ACT.Exp).then_inc(s.act_to_dve, 1)
                    act.wait_ge(s.pe_to_act, n.up(s.pe_to_act))
                    act.activation(zkt[:, :, :], B7[:, :].rearrange("p (t k) -> p t k", t=TT), ACT.Copy)\
                        .then_inc(s.act_to_pe, 1)
                    act.wait_ge(s.pe_to_act, n.up(s.pe_to_act))
                    act.activation(sq[:, 0, :], B6[:, :], ACT.Square).then_inc(s.act_to_pe, 1)
                    act.wait_ge(s.pe_to_act, n.up(s.pe_to_act))
                    act.activation(rstd[:, :], B4[:, :], ACT.Sqrt, bias=eps_rms, scale=1.0 / P).then_inc(s.act_to_dve, 1)
                out_tiles(4, 2)
                root(1.0 / D, eps_rms)

            def ffn(ada=False):
                if ada:
                    n.up(s.ada_acc, 24)
                    for k in range(2):
                        act.dma_start(adw_c[k][:, :], ada_unit(24 + k)).then_inc(ada_in[k], 16)
                swiglu_in(FF_PARTS[0], 24 if ada else None)
                read(8, 1, ACT.Copy, lambda k: m[:, k, :])
                if ada:
                    for k in range(2):
                        load_ada(k, 38 + k)
                swiglu_in(FF_PARTS[1], 38 if ada else None)
                for k in range(DC):
                    act.wait_ge(s.mm, n.up(s.mm))
                    split_next()
                    act.wait_ge(s.ev_d, n.up(s.ev_d) + 4)
                    if k >= 2:
                        act.wait_ge(s.ss_mm, n.up(s.ss_mm))
                    act.activation(sq[:, k % 2, :], m[:, k, :], ACT.Square).then_inc(s.sq_ok, 1)
                act.wait_ge(s.ss_mm, n.up(s.ss_mm, 2))
                tile[0] += DC
                root(1.0 / D, eps_rms)

            def attention(steps):
                turn = []

                def read_out():
                    while turn:
                        q = turn.pop()
                        act.wait_ge(s.ot_mm, n.up(s.ot_mm))
                        act.activation(q.Y[:, 0:q.nout, q.j * P:(q.j + 1) * P],
                                       LB[3][:, 0:q.nout * P].rearrange("p (k t) -> p k t", k=q.nout), ACT.Copy)\
                            .then_inc(s.yt_ok, 1)

                for i in range(len(steps) + 3):
                    if i >= 3 and steps[i - 3].last:
                        turn.append(steps[i - 3])
                    read_out()
                    if 1 <= i <= len(steps):
                        q = steps[i - 1]
                        nb = q.w // P
                        act.wait_ge(s.tr_mm, n.up(s.tr_mm))
                        for b in range(0, min(nb, 9), 8):
                            k = min(4, nb - b)
                            cp = act.activation(q.PT[(i - 1) % 2][:, b:b + k, :], (B4, B5, B6)[b // 4][:, 0:k * P]
                                                .rearrange("p (b t) -> p b t", b=k), ACT.Copy)
                        cp.then_inc(s.pt_a, 1)
                    if i < len(steps):
                        q = steps[i]
                        act.wait_ge(s.mx_ok, n.up(s.mx_ok))
                        act.activation(q.S[:, i % 2, 0:q.w], q.S[:, i % 2, 0:q.w], ACT.Exp,
                                       bias=mmax[:, i % 2:i % 2 + 1], accum_out=rsum[:, i % 2:i % 2 + 1])\
                            .then_inc(s.pr_ok, 1)

            def load_bias():
                act.wait_ge(s.x_ok, n.at(s.x_ok) + 1)
                act.dma_start(onehot[0:33, :], a["onehot"]).then_inc(s.extra_in, 16)
                act.dma_start(relb[0:33, :], a["relb"]).then_inc(s.extra_in, 16)

            def write_bias():
                act.wait_ge(s.bias_ok, 6)
                for g in range(3):
                    for h in range(8):
                        act.dma_start(scratch.ap()[g, h:h + 1, :, :],
                                      biasr[h:h + 1, g, :].unsqueeze(1).broadcast_to([1, P, BIAS_PITCH]))\
                            .then_inc(s.scr_out, 16)

            def dilated_mixer():
                for hp in range(4):
                    act.wait_ge(s.scr_out, 16 * 24)
                    if hp:
                        act.wait_ge(s.sc_rd, 8 * hp)
                    for hh in range(2):
                        for g in range(3):
                            src = bass.AP(tensor=scratch, offset=((g * 8 + 2 * hp + hh) * P * BIAS_PITCH) + P - 1,
                                          ap=[[BIAS_PITCH - 1, P], [1, T]])
                            act.dma_start(toep[:, 3 * hh + g, :], src).then_inc(s.toep_in, 16)
                    read(3, 2, ACT.Copy, lambda k: qk[:, k // 2 + 3 * (k % 2), :])
                    t0 = tile[0]
                    for k in range(8):
                        act.wait_ge(s.mm, n.up(s.mm))
                        if k % 4 == 3:
                            split_next()
                        b = LB[(t0 + k) % 4]
                        if k < 4:
                            act.activation(vt[:, 0:2, k, :], b[:, 0:256].rearrange("p (g e) -> p g e", g=2), ACT.Copy)\
                                .then_inc(s.ev_a, 1)
                        else:
                            act.activation(vt[:, 2, k - 4, :], b[:, 0:P], ACT.Copy).then_inc(s.ev_a, 1)
                        n.up(s.ev_a)
                    tile[0] += 8
                    attention(heads_pair(hp))
                out_tiles(2, 4)
                root(1.0 / D, eps_rms)

            def z_squares(per, bias, again):
                for k in range(DC):
                    act.wait_ge(s.mm, n.up(s.mm))
                    if k % per == per - 1:
                        split_next()
                    act.wait_ge(s.ev_d, n.up(s.ev_d) + 4)
                    if k >= 2:
                        act.wait_ge(s.ss_mm, n.up(s.ss_mm))
                    act.activation(sq[:, k % 2, :], m[:, k, :], ACT.Square).then_inc(s.sq_ok, 1)
                act.wait_ge(s.ss_mm, n.up(s.ss_mm, 2))
                tile[0] += DC
                act.activation(sq[:, 0, :], B5[:, :], ACT.Copy, scale=1.0 / D).then_inc(s.av, 1)
                act.activation(sq[:, 1, :], B5[:, :], ACT.Square, scale=1.0 / D).then_inc(s.act_to_dve, 1)
                n.up(s.av)
                act.wait_ge(s.dve_to_act, n.up(s.dve_to_act))
                act.activation(rstd[:, :], rstd[:, :], ACT.Sqrt, bias=eps_ln).then_inc(s.rms_ok, 1)
                for c in range(DC):
                    act.wait_ge(s.nb_ok, n.up(s.nb_ok))
                    if again:
                        act.activation(hhi[:, c, :], tmp[:, c % 2, :], ACT.Identity, bias=bias(c)).then_inc(s.hi_ok, 1)
                    act.activation(x[:, c, :], tmp[:, c % 2, :], ACT.Identity, bias=bias(c)).then_inc(s.x_ok, 1)

            def sparse_mixer():
                read(2, 2, ACT.Copy, lambda k: qk[:, k, :])
                read(1, 4, ACT.Copy, lambda k: vi[:, k, :], P)
                act.activation(small[:, 12:16], vec("lam", 0, 4), ACT.Abs).then_inc(s.av, 1)
                act.wait_ge(s.av, n.up(s.av))
                act.activation(small[:, 12:16], small[:, 12:16], ACT.Exp, scale=-1.0).then_inc(s.act_to_dve, 1)
                for k in range((TT - 1) * IDX_H):
                    act.wait_ge(s.pe_to_act, n.up(s.pe_to_act))
                    if k >= 2:
                        act.wait_ge(s.dve_to_act, n.up(s.dve_to_act))
                    w = P * (k // IDX_H + 2)
                    act.activation(tmp[:, k % 2, 0:w], (B4, B5)[k % 2][:, 0:w], ACT.Relu, scale=1.0 / 16)\
                        .then_inc(s.rl_ok, 1)
                act.wait_ge(s.dve_to_act, n.up(s.dve_to_act, 2))
                read(2, 2, ACT.Copy, lambda k: qk[:, 4 + k, :])
                read(2, 2, ACT.Copy, lambda k: xr[:, k, :])
                read(2, 2, ACT.Copy, lambda k: yr[:, k, :])
                for t in range(4):
                    act.wait_ge(s.pe_to_act, n.up(s.pe_to_act))
                    act.activation(rg[:, 1, :], B4[:, :], ACT.Sigmoid, bias=vec("ga_b", t)).then_inc(s.av, 1)
                    act.activation(rg[:, 2, :], B5[:, :], ACT.Sigmoid, bias=vec("gx_b", t)).then_inc(s.act_to_dve, 1)
                    n.up(s.av)
                    act.activation(rg[:, 6, :], yr[:, t, :], ACT.Square).then_inc(s.act_to_dve, 1)
                    act.wait_ge(s.dve_to_act, n.up(s.dve_to_act))
                    act.activation(rg[:, 3, :], rg[:, 1, :], ACT.Exp).then_inc(s.av, 1)
                    act.activation(rg[:, 4, :], rg[:, 1, :], ACT.Tanh, scale=-1.0).then_inc(s.av, 1)
                    act.wait_ge(s.av, n.up(s.av, 2))
                    act.activation(rg[:, 5, :], rg[:, 3, :], ACT.Square).then_inc(s.act_to_dve, 1)
                    act.wait_ge(s.dve_to_act, n.up(s.dve_to_act))
                    act.activation(rg[:, 6, :], rg[:, 6, :], ACT.Tanh, scale=0.7978845608028654).then_inc(s.act_to_dve, 1)
                    act.wait_ge(s.dve_to_act, n.up(s.dve_to_act))
                    act.activation(rg[:, 5, :], rg[:, 5, :], ACT.Sqrt).then_inc(s.act_to_dve, 1)
                attention(sparse_steps())
                z_squares(2, lambda c: vec("ln1_b", c), stop > 5)

            def mla_mixer():
                t0 = tile[0]
                read(3, 2, ACT.Copy, lambda k: m[:, k, :])
                read(1, 1, ACT.Copy, lambda k: krr)
                act.wait_ge(s.ev_a, n.at(s.ev_a) + 4)
                for c in range(6):
                    if c >= 2:
                        act.wait_ge(s.ss_mm, n.up(s.ss_mm))
                    act.activation(sq[:, c % 2, :], m[:, c, :], ACT.Square).then_inc(s.sq_ok, 1)
                act.wait_ge(s.ss_mm, n.up(s.ss_mm, 2))
                act.activation(rstd[:, :], B4[:, :], ACT.Sqrt, bias=eps_rms, scale=1.0 / 512).then_inc(s.rms_ok, 1)
                act.activation(sq[:, 0, :], B5[:, :], ACT.Sqrt, bias=eps_rms, scale=1.0 / 256).then_inc(s.rms_ok, 1)
                for g in range(4):
                    t0 = tile[0]
                    for k in range(9):
                        act.wait_ge(s.mm, n.up(s.mm))
                        if k in (2, 8):
                            split_next()
                        b = LB[(t0 + k) % 4]
                        if k in (0, 1, 3, 4):
                            at = 2 * k if k < 2 else 2 * k - 2
                            act.activation(qk[0:64, at, :], b[0:64, :], ACT.Copy).then_inc(s.av, 1)
                            n.up(s.av)
                            act.activation(qk[0:64, at + 1, :], b[64:P, :], ACT.Copy).then_inc(s.ev_a, 1)
                        elif k == 2:
                            act.activation(qrr, b[:, :], ACT.Copy).then_inc(s.ev_a, 1)
                        else:
                            act.activation(vm[:, k - 5, :], b[:, 0:256], ACT.Copy).then_inc(s.ev_a, 1)
                        n.up(s.ev_a)
                    tile[0] += 9
                    attention(mla_steps(g))
                z_squares(2, lambda c: vec("ln1_b", 8 + c), stop > 7)

            def mlp(i):
                act.dma_start(pin[:, :, :], a["p"][i]).then_inc(s.p_in, 16)
                read(4, 2, ACT.Sigmoid, lambda k: m[:, k, :])
                for _ in range(2):
                    act.wait_ge(s.mm, n.up(s.mm, 4))
                    split_next()
                tile[0] += 8
                n.up(s.ev_d, 8)
                for part in range(2):
                    t0 = tile[0]
                    rounds = 3

                    def relu_unit(t0, j, last):
                        for t in range(2):
                            act.wait_ge(s.mm, n.up(s.mm))
                            if t == 1 and not last:
                                split((st.u + j) % 2, UNIT)
                            elif t == 1:
                                split_next()
                            act.wait_ge(s.sa_free, n.up(s.sa_free))
                            act.activation(tmp[:, t, :], LB[(t0 + 2 * j + t) % 4][:, :], ACT.Relu).then_inc(s.ev_a, 1)
                            n.up(s.ev_a)

                    with n.loop(act, rounds, {s.mm: 4, s.sa_free: 4, s.ev_a: 4, s_raw[0]: 16, s_raw[1]: 16}):
                        for j in range(2):
                            relu_unit(t0, j, False)
                    st.u += 2 * rounds
                    for j in range(2):
                        relu_unit(t0, j, True)
                    tile[0] += 16
                    if part == 0:
                        for _ in range(8):
                            act.wait_ge(s.mm, n.up(s.mm))
                            split_next()
                        tile[0] += 8
                        n.up(s.ev_d, 8)
                z_squares(1, lambda c: vec("ln2_b", 8 * i + c), i == 0 and stop > 6)

            act.wait_ge(s.vecs_in, 16)
            act.wait_ge(s.ready, 1)
            act.activation(silu_c, vec("c", 0, 8), ACT.Silu).then_inc(s.silu_ok, 1)
            for u in range(2):
                split(u, plan[u][1] * plan[u][2])
            act.wait_ge(s.x_in, 16)
            pre_norm(0, None)
            hgrn_mixer()
            if stop > 1:
                pre_norm(1)
                ffn(True)
            if stop > 2:
                load_bias()
                pre_norm(2)
                write_bias()
                dilated_mixer()
            if stop > 3:
                pre_norm(3)
                ffn()
            if stop > 4:
                sparse_mixer()
            if stop > 5:
                mlp(0)
            if stop > 6:
                mla_mixer()
            if stop > 7:
                mlp(1)

        @block.vector
        def _(v):
            n = Counts()
            tile = [0]

            def chain(ins):
                ins.then_inc(s.dv, 1)
                v.wait_ge(s.dv, n.up(s.dv))

            def split_chunk(src, dst, done):
                hi, lo = dst
                chain(v.tensor_copy(hi, src))
                v.tensor_tensor(lo, src, hi.bitcast(F32), ALU.subtract).then_inc(done, 1)
                n.up(done)

            def recip():
                v.wait_ge(s.rms_ok, n.up(s.rms_ok))
                chain(v.reciprocal(rstd[:, :], rstd[:, :]))

            def pre_norm(ls):
                recip()
                for c in range(DC):
                    if c >= 2:
                        v.wait_ge(s.h_ok, n.at(s.h_ok))
                    v.scalar_tensor_tensor(tmp[:, c % 2, :], x[:, c, :], mods[:, ls, 8 + c:9 + c], rstd[:, :],
                                           ALU.mult, ALU.mult).then_inc(s.nb_ok, 1)
                    if c:
                        low_part(c - 1, mods[:, ls, c - 1:c])
                low_part(DC - 1, mods[:, ls, DC - 1:DC])

            def low_part(c, shift):
                v.wait_ge(s.hi_ok, n.up(s.hi_ok))
                v.scalar_tensor_tensor(hlo[:, c, :], tmp[:, c % 2, :], shift, hhi[:, c, :].bitcast(F32),
                                       ALU.add, ALU.subtract).then_inc(s.h_ok, 1)
                n.up(s.h_ok)

            def post_norm(ls):
                recip()
                for c in range(DC):
                    b = tmp[:, c % 2, :]
                    chain(v.tensor_tensor(b, m[:, c, :], rstd[:, :], ALU.mult))
                    v.scalar_tensor_tensor(x[:, c, :], b, mods[:, ls, 16 + c:17 + c], x[:, c, :], ALU.mult, ALU.add)\
                        .then_inc(s.x_ok, 1)
                v.wait_ge(s.x_ok, n.up(s.x_ok, 8))

            def ada_products(slot, landed, k, acc=acc):
                v.wait_ge(landed, n.up(landed, 16))
                v.wait_ge(s.ada_mm, n.up(s.ada_mm))
                b = acc[:, k % 2, :]
                chain(v.tensor_scalar(b, slot[:, 0:256], silu_c[:, 0:1], None, ALU.mult))
                for c in range(1, DC):
                    ins = v.scalar_tensor_tensor(b, slot[:, c * 256:c * 256 + 256], silu_c[:, c:c + 1], b,
                                                 ALU.mult, ALU.add)
                    if c < DC - 1:
                        chain(ins)
                ins.then_inc(s.ada_acc, 1)

            def modulation(l0, nl):
                v.wait_ge(s.ada_mm, n.at(s.ada_mm) + 2)
                md = mods[:, l0:l0 + nl, :]
                chain(v.tensor_tensor(md, B5[:, 0:24 * nl].rearrange("p (l f) -> p l f", l=nl),
                                      vec("ada_b", 24 * l0, 24 * nl).rearrange("p (l f) -> p l f", l=nl), ALU.add))
                chain(v.scalar_tensor_tensor(md[:, :, 8:16], md[:, :, 8:16], 1.0,
                                             vec("norm_pre", 8 * l0, 8 * nl).rearrange("p (l f) -> p l f", l=nl),
                                             ALU.add, ALU.mult))
                chain(v.tensor_tensor(md[:, :, 16:24], md[:, :, 16:24],
                                      vec("norm_post", 8 * l0, 8 * nl).rearrange("p (l f) -> p l f", l=nl), ALU.mult))

            def skip(k):
                n.up(s.mm, k)
                n.up(s.ev_a, k)
                tile[0] += k

            def halves(ap, m_):
                return ap.rearrange("p (b two j) -> p b two j", two=2, j=m_)

            def hgrn_mixer():
                for k in range(12):
                    ada_products(adw_b[k % 4], ada_b_in[k % 4], k)
                modulation(1, 1)
                skip(24)
                for h in range(HGRN_H):
                    v.wait_ge(s.act_to_dve, n.up(s.act_to_dve))
                    b = tmp[:, h % 2, :]
                    chain(v.scalar_tensor_tensor(b, zk[:, h, :], 0.0, b, ALU.min, ALU.subtract))
                    chain(v.tensor_tensor_scan(zb[:, h, :], con("reset"), b, 0.0, ALU.mult, ALU.add))
                    v.tensor_tensor(zk[:, h, :], b, zk[:, h, :], ALU.subtract).then_inc(s.dve_to_act, 1)
                v.wait_ge(s.act_to_dve, n.up(s.act_to_dve, 4))
                v.wait_ge(s.ev_a, n.at(s.ev_a) + 4)
                for g, win in enumerate(POOL_WINDOWS):
                    src, k, w = zu[:, g, :], 1, 0
                    bufs = (tmp[:, 0, :], tmp[:, 1, :])
                    while k < win:
                        dst = bufs[w % 2]
                        v.tensor_copy(dst[:, 0:k], src[:, 0:k]).then_inc(s.dv, 1)
                        n.up(s.dv)
                        chain(v.tensor_tensor(dst[:, k:T], src[:, k:T], src[:, 0:T - k], ALU.add))
                        src, k, w = dst, 2 * k, w + 1
                    if g >= 2:
                        v.wait_ge(s.pe_to_dve, n.up(s.pe_to_dve))
                        chain(v.tensor_scalar(zt[:, :, :].rearrange("p t k -> p (t k)"), (B4, B5)[g % 2][:, :],
                                              vec("pool_scale", g - 2), None, ALU.mult))
                        split_chunk(zt[:, :, :].rearrange("p t k -> p (t k)"), hidden(g - 2), s.y_ok)
                    d = zw[:, g % 2, :]
                    v.tensor_tensor(d[:, 0:16], src[:, 0:16], con("inv", 16 * g, 16), ALU.mult).then_inc(s.dv, 1)
                    n.up(s.dv)
                    chain(v.tensor_scalar(d[:, 16:T], src[:, 16:T], 1.0 / win, None, ALU.mult))
                    v.tensor_tensor(d, d, zu[:, g, :], ALU.subtract).then_inc(s.dve_to_pe, 1)
                    n.up(s.dve_to_pe)
                for g in range(2, 4):
                    v.wait_ge(s.pe_to_dve, n.up(s.pe_to_dve))
                    v.wait_ge(s.y_ok, n.at(s.y_ok))
                    chain(v.tensor_scalar(zt[:, :, :].rearrange("p t k -> p (t k)"), (B4, B5)[g % 2][:, :],
                                          vec("pool_scale", g), None, ALU.mult))
                    split_chunk(zt[:, :, :].rearrange("p t k -> p (t k)"), hidden(g), s.y_ok)
                for h in range(HGRN_H):
                    v.wait_ge(s.y_ok, n.at(s.y_ok))
                    b = zb[:, h, :]
                    L = len(LEVELS)

                    def exponents(l):
                        e = ze[:, l % 2, :]
                        v.wait_ge(s.dve_to_pe, n.at(s.dve_to_pe))
                        if l < L:
                            k = LEVELS[l]
                            bb, ee = halves(b, k), halves(e, k)
                            r = bb[:, :, 0, k - 1:k].broadcast_to([P, T // (2 * k), k])
                            v.tensor_tensor(ee[:, :, 1, :], bb[:, :, 1, :], r, ALU.subtract).then_inc(s.dv, 1)
                            n.up(s.dv)
                            v.tensor_tensor(ee[:, :, 0, :], r, bb[:, :, 0, :], ALU.subtract).then_inc(s.dve_to_act, 1)
                        elif l == L:
                            v.tensor_copy(e, b).then_inc(s.dve_to_act, 1)
                        else:
                            bt, et = (y.rearrange("p (t j) -> p t j", t=TT) for y in (b, e))
                            end = bt[:, :, P - 1:P].broadcast_to([P, TT, P])
                            v.tensor_tensor(et, end, bt, ALU.subtract).then_inc(s.dve_to_act, 1)

                    def collect(l, done=s.dv):
                        v.wait_ge(s.pe_to_dve, n.up(s.pe_to_dve))
                        ps = (B4, B5)[l % 2][:, :].rearrange("p (t j) -> p t j", t=TT)
                        mask = (con("level", l * P, P) if l < L else ident).unsqueeze(1).broadcast_to([P, TT, P])
                        if l == 0:
                            chain(v.tensor_tensor(za[:, :, :], ps, mask, ALU.mult))
                        else:
                            chain(v.tensor_tensor(zt[:, :, :], ps, mask, ALU.mult))
                            v.tensor_tensor(za[:, :, :], za[:, :, :], zt[:, :, :], ALU.add).then_inc(done, 1)
                            v.wait_ge(done, n.up(done))

                    exponents(0)
                    for l in range(L):
                        exponents(l + 1)
                        v.wait_ge(s.act_to_dve, n.up(s.act_to_dve))
                        e = ze[:, l % 2, :]
                        eh, qh, kh, qd, kd = (halves(y, LEVELS[l]) for y in (
                            e, zq[:, h, :], zk[:, h, :], zqe[:, l % 2, :], zke[:, l % 2, :]))
                        qn, kn = (slice(1, 2), slice(0, 1)) if h or l >= 2 else (slice(0, 2), slice(0, 2))
                        v.tensor_tensor(qd[:, :, qn, :], qh[:, :, qn, :], eh[:, :, qn, :], ALU.mult).then_inc(s.dv, 1)
                        n.up(s.dv)
                        v.tensor_tensor(kd[:, :, kn, :], kh[:, :, kn, :], eh[:, :, kn, :], ALU.mult)\
                            .then_inc(s.dve_to_pe, 1)
                        n.up(s.dve_to_pe)
                        if l:
                            collect(l - 1, s.dve_to_pe if l == L - 1 else s.dv)
                    collect(L - 1)
                    exponents(L + 1)
                    v.wait_ge(s.act_to_dve, n.up(s.act_to_dve))
                    e = ze[:, L % 2, :]
                    collect(L)
                    chain(v.tensor_tensor(zqe[:, 1, :], zq[:, h, :], e, ALU.mult))
                    chain(v.tensor_copy(decay, e.rearrange("p (t j) -> p t j", t=TT)[:, :, P - 1:P]))
                    v.wait_ge(s.act_to_dve, n.up(s.act_to_dve))
                    v.tensor_tensor(zke[:, 0, :], zk[:, h, :], ze[:, (L + 1) % 2, :], ALU.mult).then_inc(s.dve_to_pe, 1)
                    v.wait_ge(s.dve_to_pe, n.up(s.dve_to_pe))
                    v.wait_ge(s.pe_to_dve, n.up(s.pe_to_dve))
                    chain(v.tensor_copy(zs[:, 0, :], B7[:, 0:P]))
                    chain(v.scalar_tensor_tensor(zs[:, 1, :], zs[:, 0, :], decay[:, 1:2], B7[:, P:2 * P],
                                                 ALU.mult, ALU.add))
                    v.scalar_tensor_tensor(zs[:, 2, :], zs[:, 1, :], decay[:, 2:3], B7[:, 2 * P:3 * P],
                                           ALU.mult, ALU.add).then_inc(s.dve_to_pe, 1)
                    n.up(s.dve_to_pe)
                    v.wait_ge(s.act_to_dve, n.up(s.act_to_dve))
                    chain(v.reciprocal(rstd[:, :], rstd[:, :]))
                    chain(v.tensor_tensor(tmp[:, 0, :], B6[:, :], rstd[:, :], ALU.mult))
                    chain(v.scalar_tensor_tensor(tmp[:, 0, :], tmp[:, 0, :], vec("out_norm"), zg[:, h, :],
                                                 ALU.mult, ALU.mult))
                    split_chunk(tmp[:, 0, :], hidden(4 + h), s.y_ok)
                n.up(s.dve_to_act, HGRN_H * (1 + len(LEVELS) + 2))
                skip(8)

            def swiglu_in(size, ada=False):
                t0 = tile[0]
                moved = {s.mm: 4, s.sa_ok: 2, s.dv: 2, s.ev_d: 4}
                if ada:
                    moved.update({s.dv: 2 + 2 * (DC - 1), s.ada_mm: 2, ada_in[0]: 16, ada_in[1]: 16})
                with n.loop(v, size // 2, moved) as i:
                    for j in range(2):
                        if ada:
                            ada_products(adw_c[j], ada_in[j], j)
                        v.wait_ge(s.sa_ok, n.up(s.sa_ok))
                        v.wait_ge(s.mm, n.up(s.mm, 2))
                        v.tensor_tensor(sq[:, j, :], tmp[:, j, :], LB[(t0 + 2 * j + 1) % 4][:, :], ALU.mult)\
                            .then_inc(s.ev_d, 2)
                        v.wait_ge(s.ev_d, n.up(s.ev_d, 2) + 4)
                        hi, lo = (q[:, bass.ds(i * 2 + j, 1), :].rearrange("p a t -> p (a t)") for q in (ghi, glo))
                        chain(v.tensor_copy(hi, sq[:, j, :]))
                        v.tensor_tensor(lo, sq[:, j, :], hi.bitcast(F32), ALU.subtract).then_inc(s.y_ok, 1)
                tile[0] += 2 * size

            def ffn(ls, ada=False):
                pre_norm(ls)
                swiglu_in(FF_PARTS[0], ada)
                if ada:
                    for k in range(2):
                        ada_products(adw_c[k], ada_in[k], k)
                skip(8)
                swiglu_in(FF_PARTS[1], ada)
                if ada:
                    modulation(2, 2)
                for k in range(DC):
                    v.wait_ge(s.mm, n.up(s.mm))
                    v.tensor_tensor(m[:, k, :], m[:, k, :], LB[(tile[0] + k) % 4][:, :], ALU.add)\
                        .then_inc(s.ev_d, 1)
                    n.up(s.ev_d)
                tile[0] += DC
                post_norm(ls)

            def bias_rows():
                for g in range(3):
                    for k in range(2):
                        v.wait_ge(s.bias_mm, n.up(s.bias_mm))
                        v.tensor_copy(biasr[0:8, g, k * 320:(k + 1) * 320], (LB + [B6, B7])[2 * g + k][0:8, 0:320])\
                            .then_inc(s.bias_ok, 1)

            def attention(steps):
                for i in range(len(steps) + 3):
                    if i < len(steps):
                        q = steps[i]
                        if q.slope is not None:
                            v.scalar_tensor_tensor(bh[:, 0:q.w], q.slope[1], q.slope[0], q.slope[2],
                                                   ALU.mult, ALU.add).then_inc(s.dv, 1)
                            v.wait_ge(s.dv, n.up(s.dv))
                        v.wait_ge(s.sc_mm, n.up(s.sc_mm))
                        for k, (bank, at, w, add, _) in enumerate(q.adds):
                            done = s.sc_rd if k == len(q.adds) - 1 else s.dv
                            src = bank[:, at:at + w] if len(q.adds) < 3 else bank[:, 0:w]
                            if add is None:
                                v.tensor_scalar(q.S[:, i % 2, at:at + w], src, q.scale, None, ALU.mult)\
                                    .then_inc(done, 1)
                            else:
                                v.scalar_tensor_tensor(q.S[:, i % 2, at:at + w], src, q.scale, add,
                                                       ALU.mult, ALU.add).then_inc(done, 1)
                            n.up(done)
                        v.wait_ge(s.sc_rd, n.at(s.sc_rd))
                        v.tensor_reduce(mmax[:, i % 2:i % 2 + 1], q.S[:, i % 2, 0:q.w], AX_X, ALU.max, negate=True)\
                            .then_inc(s.mx_ok, 1)
                        n.up(s.mx_ok)
                    if 2 <= i < len(steps) + 2 and steps[i - 2].last:
                        q = steps[i - 2]
                        nh = q.col // 64 + 1
                        v.wait_ge(s.pv_mm, n.up(s.pv_mm))
                        v.wait_ge(s.dv, n.at(s.dv))
                        v.tensor_tensor(q.O[:, 0:64 * nh].rearrange("p (h e) -> p h e", h=nh),
                                        B7[:, 0:64 * nh].rearrange("p (h e) -> p h e", h=nh),
                                        rinv8[:, 0:nh].unsqueeze(2).broadcast_to([P, nh, 64]), ALU.mult)\
                            .then_inc(s.o_ok, 1)
                        v.wait_ge(s.o_ok, n.up(s.o_ok))
                    if 1 <= i <= len(steps):
                        q = steps[i - 1]
                        nb = q.w // P
                        v.wait_ge(s.pr_ok, n.up(s.pr_ok))
                        v.reciprocal(rinv8[:, q.col // 64:q.col // 64 + 1], rsum[:, (i - 1) % 2:(i - 1) % 2 + 1])\
                            .then_inc(s.dv, 1)
                        n.up(s.dv)
                        v.wait_ge(s.tr_mm, n.up(s.tr_mm))
                        if nb > 4:
                            k = min(4, nb - 4)
                            v.tensor_copy(q.PT[(i - 1) % 2][:, 4:4 + k, :], B5[:, 0:k * P].rearrange("p (b t) -> p b t", b=k))\
                                .then_inc(s.pt_d, 1)
                        else:
                            v.tensor_copy(small[:, 28:29], small[:, 11:12]).then_inc(s.pt_d, 1)
                        n.up(s.pt_d)
                    if i >= 3 and steps[i - 3].last:
                        q = steps[i - 3]
                        v.wait_ge(s.yt_ok, n.up(s.yt_ok))
                        if q.j == TT - 1:
                            for k in range(q.nout):
                                split_chunk(q.Y[:, k, :], hidden(q.chunk + k), s.y_ok)
                v.wait_ge(s.y_ok, n.at(s.y_ok))

            def dilated_mixer(ls):
                pre_norm(ls)
                for hp in range(4):
                    skip(14)
                    v.wait_ge(s.toep_in, n.up(s.toep_in, 96))
                    attention(heads_pair(hp))
                skip(8)
                post_norm(ls)

            def add_tiles(fresh):
                for k in range(DC):
                    v.wait_ge(s.mm, n.up(s.mm))
                    b = LB[(tile[0] + k) % 4]
                    if fresh:
                        v.scalar_tensor_tensor(m[:, k, :], x[:, k, :], ALPHA, b[:, :], ALU.mult, ALU.add)\
                            .then_inc(s.ev_d, 1)
                    else:
                        chain(v.tensor_tensor(m[:, k, :], m[:, k, :], b[:, :], ALU.add))
                        v.scalar_tensor_tensor(m[:, k, :], x[:, k, :], ALPHA, m[:, k, :], ALU.mult, ALU.add)\
                            .then_inc(s.ev_d, 1)
                    n.up(s.ev_d)
                tile[0] += DC

            def layer_norm(g, b, i, again):
                v.wait_ge(s.act_to_dve, n.up(s.act_to_dve))
                v.scalar_tensor_tensor(rstd[:, :], B4[:, :], 1.0 / D, sq[:, 1, :], ALU.mult, ALU.subtract)\
                    .then_inc(s.dve_to_act, 1)
                recip()
                for c in range(DC):
                    y = tmp[:, c % 2, :]
                    if c >= 2:
                        v.wait_ge(s.x_ok, n.up(s.x_ok))
                        v.wait_ge(s.h_ok, n.at(s.h_ok))
                    chain(v.tensor_tensor(y, m[:, c, :], sq[:, 0, :], ALU.subtract))
                    v.scalar_tensor_tensor(y, y, vec(g, 8 * i + c), rstd[:, :], ALU.mult, ALU.mult).then_inc(s.nb_ok, 1)
                    if again and c:
                        low_part(c - 1, vec(b, 8 * i + c - 1))
                if again:
                    low_part(DC - 1, vec(b, 8 * i + DC - 1))
                v.wait_ge(s.x_ok, n.up(s.x_ok, 2))

            def log_decay_scale():
                e, q, w = small[:, 12:16], small[:, 28:32], small[:, 36:40]
                v.wait_ge(s.act_to_dve, n.up(s.act_to_dve))
                chain(v.tensor_scalar(q, e, 2.0, None, ALU.add))
                chain(v.reciprocal(q, q))
                chain(v.tensor_tensor(e, e, q, ALU.mult))
                chain(v.tensor_tensor(q, e, e, ALU.mult))
                chain(v.tensor_scalar(w, q, 1.0 / 15, 1.0 / 13, ALU.mult, ALU.add))
                for k in (11, 9, 7, 5, 3, 1):
                    chain(v.tensor_tensor(w, w, q, ALU.mult))
                    chain(v.tensor_scalar(w, w, 1.0 / k, None, ALU.add))
                chain(v.tensor_tensor(e, e, w, ALU.mult))
                chain(v.tensor_scalar(q, vec("lam", 0, 4), -1.0, 0.0, ALU.mult, ALU.max))
                chain(v.scalar_tensor_tensor(e, e, 2.0, q, ALU.mult, ALU.add))
                chain(v.tensor_scalar(e, e, -8.0, None, ALU.mult))

            def sparse_mixer():
                for c in range(DC):
                    split_chunk(x[:, c, :], hin(c), s.h_ok)
                skip(20)
                log_decay_scale()
                for j in range(1, TT):
                    w, off = P * (j + 1), P * (0, 0, 2, 5)[j]
                    isc = msk[:, off:off + w]
                    for h in range(IDX_H):
                        k = (j - 1) * IDX_H + h
                        v.wait_ge(s.rl_ok, n.up(s.rl_ok))
                        b, wt = tmp[:, k % 2, 0:w], vi[:, j, 64 + h:65 + h]
                        if h == 0:
                            v.tensor_scalar(isc, b, wt, None, ALU.mult).then_inc(s.dve_to_act, 1)
                        else:
                            v.scalar_tensor_tensor(isc, b, wt, isc, ALU.mult, ALU.add).then_inc(s.dve_to_act, 1)
                        n.up(s.dve_to_act)
                        v.wait_ge(s.dve_to_act, n.at(s.dve_to_act))
                for j in range(1, TT):
                    w, off = P * (j + 1), P * (0, 0, 2, 5)[j]
                    isc, diag = msk[:, off:off + w], msk[:, off + w - P:off + w]
                    chain(v.tensor_tensor(diag, diag, con("causal"), ALU.add))
                    for _ in range(TOPK // 8):
                        chain(v.max(top8, isc))
                        chain(v.match_replace(isc, top8, isc, TAKEN))
                    chain(v.tensor_scalar(isc, isc, TAKEN / 2, NEG, ALU.is_gt, ALU.mult))
                v.wait_ge(s.ev_a, n.at(s.ev_a) + 4)
                for t in range(4):
                    xc, r_, ig, a_, th, w_, gt, hs = (rg[:, k, :] for k in range(8))
                    cw = lambda k: vec("conv_w", 4 * k + t)
                    chain(v.tensor_scalar(xc, xr[:, t, :], cw(3), vec("conv_b", t), ALU.mult, ALU.add))
                    for k in range(3):
                        d = 3 - k
                        ins = v.scalar_tensor_tensor(xc[:, d:T], xr[:, t, 0:T - d], cw(k), xc[:, d:T],
                                                     ALU.mult, ALU.add)
                        if k < 2:
                            chain(ins)
                    ins.then_inc(s.dve_to_pe, 1)
                    v.wait_ge(s.dve_to_pe, n.up(s.dve_to_pe))
                    v.wait_ge(s.act_to_dve, n.up(s.act_to_dve))
                    v.tensor_scalar(r_, r_, spl[:, t:t + 1], None, ALU.mult).then_inc(s.dve_to_act, 1)
                    n.up(s.dve_to_act)
                    chain(v.tensor_tensor(ig, ig, xc, ALU.mult))
                    v.wait_ge(s.act_to_dve, n.up(s.act_to_dve))
                    chain(v.tensor_scalar(gt, gt, 0.044715, 1.0, ALU.mult, ALU.add))
                    v.wait_ge(s.act_to_dve, n.up(s.act_to_dve))
                    v.tensor_tensor(gt, gt, yr[:, t, :], ALU.mult).then_inc(s.dve_to_act, 1)
                    n.up(s.dve_to_act)
                    v.scalar_tensor_tensor(w_, w_, 1.0, th, ALU.add, ALU.mult).then_inc(s.dve_to_act, 1)
                    n.up(s.dve_to_act)
                    v.wait_ge(s.act_to_dve, n.up(s.act_to_dve))
                    chain(v.scalar_tensor_tensor(gt, gt, 1.0, yr[:, t, :], ALU.add, ALU.mult))
                    v.wait_ge(s.act_to_dve, n.up(s.act_to_dve))
                    chain(v.tensor_tensor(w_, w_, ig, ALU.mult))
                    chain(v.tensor_tensor_scan(hs, a_, w_, 0.0, ALU.mult, ALU.add))
                    chain(v.scalar_tensor_tensor(hs, gt, 0.5, hs, ALU.mult, ALU.mult))
                    split_chunk(hs, hidden(t), s.y_ok)
                    v.wait_ge(s.y_ok, n.at(s.y_ok))
                v.tensor_copy(small[:, 28:29], small[:, 11:12]).then_inc(s.top_ok, 1)
                v.wait_ge(s.top_ok, n.up(s.top_ok))
                attention(sparse_steps())
                add_tiles(True)
                layer_norm("ln1_g", "ln1_b", 0, stop > 5)

            def rotate(first, src):
                v.wait_ge(s.pe_to_dve, n.up(s.pe_to_dve))
                chain(v.tensor_tensor(tmp[:, 0, :], B6[:, :], con("sin"), ALU.mult))
                chain(v.tensor_tensor(tmp[:, 1, :], src, con("cos"), ALU.mult))
                for h in range(4):
                    r = slice(32 * h, 32 * h + 32)
                    ins = v.tensor_tensor(qk[64:96, first + h, :], tmp[r, 0, :], tmp[r, 1, :], ALU.add)
                    if h < 3:
                        chain(ins)
                ins.then_inc(s.dve_to_pe, 1)
                v.wait_ge(s.dve_to_pe, n.up(s.dve_to_pe))

            def mla_mixer():
                skip(7)
                for c in range(6):
                    if c in (0, 4):
                        root = rstd[:, :] if c == 0 else sq[:, 0, :]
                        v.wait_ge(s.rms_ok, n.up(s.rms_ok))
                        chain(v.reciprocal(root, root))
                    gain = vec("q_norm", c) if c < 4 else vec("kv_norm", c - 4)
                    chain(v.scalar_tensor_tensor(tmp[:, c % 2, :], m[:, c, :], gain, root, ALU.mult, ALU.mult))
                    split_chunk(tmp[:, c % 2, :], hin(c), s.h_ok)
                v.wait_ge(s.h_ok, n.at(s.h_ok))
                rotate(4, krr)
                for g in range(4):
                    skip(9)
                    rotate(0, qrr)
                    attention(mla_steps(g))
                add_tiles(True)
                layer_norm("ln1_g", "ln1_b", 1, stop > 7)

            def mlp(i):
                v.wait_ge(s.p_in, n.up(s.p_in, 16))
                for c in range(2):
                    split_chunk(pin[:, c, :], hidden(14 + c), s.p_ok)
                skip(8)
                v.wait_ge(s.ev_a, n.at(s.ev_a) + 4)
                for k in range(8):
                    v.wait_ge(s.mm, n.up(s.mm))
                    v.tensor_tensor(m[:, k, :], m[:, k, :], LB[(tile[0] + k) % 4][:, :], ALU.mult)\
                        .then_inc(s.ev_d, 1)
                    n.up(s.ev_d)
                tile[0] += 8
                for part in range(2):
                    t0 = tile[0]
                    with n.loop(v, 4, {s.mm: 4, s.ev_a: 4, s.dv: 4, s.sa_free: 4}) as r:
                        for t in range(4):
                            n.up(s.mm)
                            v.wait_ge(s.ev_a, n.up(s.ev_a) + 4)
                            v.tensor_tensor(sq[:, t % 2, :], tmp[:, t % 2, :], tmp[:, t % 2, :], ALU.mult)\
                                .then_inc(s.sa_free, 1)
                            v.wait_ge(s.sa_free, n.up(s.sa_free) + 2)
                            hi, lo = (q[:, bass.ds(r * 4 + t, 1), :].rearrange("p a t -> p (a t)") for q in (ghi, glo))
                            chain(v.tensor_copy(hi, sq[:, t % 2, :]))
                            v.tensor_tensor(lo, sq[:, t % 2, :], hi.bitcast(F32), ALU.subtract).then_inc(s.y_ok, 1)
                    n.up(s.y_ok, 16)
                    tile[0] += 16
                    if part == 0:
                        for k in range(8):
                            v.wait_ge(s.mm, n.up(s.mm))
                            v.tensor_tensor(m[:, k, :], m[:, k, :], LB[(tile[0] + k) % 4][:, :], ALU.add)\
                                .then_inc(s.ev_d, 1)
                            n.up(s.ev_d)
                        tile[0] += 8
                add_tiles(False)
                layer_norm("ln2_g", "ln2_b", i, i == 0 and stop > 6)

            v.memset(small[:, 26:27], 0.0).then_inc(s.ev_d, 4)
            v.memset(small[:, 27:28], 0.0).then_inc(s.ev_a, 4)
            v.memset(small[:, 28:29], 0.0).then_inc(s.sa_free, 2)
            v.wait_ge(s.vecs_in, 16)
            v.wait_ge(s.cst_in, 16)
            v.memset(small[:, 29:30], 0.0).then_inc(s.ada_mm, 2)
            v.wait_ge(s.silu_ok, 1)
            for k in range(12):
                ada_products(adw_a[k % 6], ada_in[k % 6], k, acc_first)
            modulation(0, 1)
            pre_norm(0)
            hgrn_mixer()
            post_norm(0)
            if stop > 1:
                ffn(1, True)
            if stop > 2:
                bias_rows()
                dilated_mixer(2)
            if stop > 3:
                ffn(3)
            if stop > 4:
                sparse_mixer()
            if stop > 5:
                mlp(0)
            if stop > 6:
                mla_mixer()
            if stop > 7:
                mlp(1)


def block_of(w, rows, cols):
    return np.stack([w[r:r + P][:, cols] for r in rows], axis=1).reshape(-1)


def weight_stream(v):
    span = lambda a, k: list(range(a, a + k))
    rows = lambda c0, k: [P * (c0 + i) for i in range(k)]
    full = rows(0, DC)
    out = []

    def cols_in(w, cols, width=256, r=full):
        for k in range(0, len(cols), width):
            out.append(block_of(w, r, cols[k:k + width]))

    w = v["hyb_w_in"][0]
    cols_in(w, span(512, 512) + span(2048, 512) + span(1024, 512) + span(1536, 512) + span(0, 512))
    cols_in(v["hyb_w_out"][0], span(0, D))

    def ffn(l):
        wi, wo, c0 = v["ffn_w_in"][l], v["ffn_w_out"][l], 0
        for k in FF_PARTS:
            for c in range(c0, c0 + k):
                out.append(block_of(wi, full, span(c * P, P) + span(FF + c * P, P)))
            cols_in(wo, span(0, D), P, rows(c0, k))
            c0 += k

    def mlp(l):
        cols_in(v["ple_w_gate_2"][l], span(0, D))
        cols_in(v["ple_w_proj_2"][l], span(0, D), 512, rows(0, 2))
        c0 = 0
        for k in FF2_PARTS:
            cols_in(v["mlp_w1_2"][l], span(c0 * P, k * P))
            cols_in(v["mlp_w2_2"][l], span(0, D), P, rows(c0, k))
            c0 += k

    ffn(0)
    w = v["att_w_qkv"][0]
    for hp in range(4):
        at = lambda kind, g: span(kind * 1536 + g * 512 + hp * P, P)
        for g in range(3):
            out.append(block_of(w, full, at(0, g) + at(1, g)))
        out.append(block_of(w, full, at(2, 0) + at(2, 1)))
        out.append(block_of(w, full, at(2, 2)))
    cols_in(v["att_w_out"][0], span(0, D), 512, rows(0, 4))
    ffn(1)
    w = v["hy_w_in_2"][0]
    w = np.concatenate([w, np.zeros((D, 60), w.dtype)], axis=1)
    q, k, vv, iq, ik, iw = 1024, 1536, 1600, 1664, 1920, 1984
    out.append(block_of(w, full, span(iq, 256)))
    out.append(block_of(w, full, span(ik, 64) * 2 + span(k, 64) * 2))
    out.append(block_of(w, full, span(vv, 64) + span(iw, 64)))
    cols_in(w, span(q, 512) + span(0, 512) + span(512, 512))
    cols_in(v["hy_w_out_2"][0], span(0, D))
    mlp(0)
    w = v["mla_w_down_2"][0]
    cols_in(w, span(0, 768))
    out.append(block_of(w, full, span(768, 32) * 4))
    wq, wkv = v["mla_w_uq_2"][0], v["mla_w_ukv_2"][0]
    for g in range(4):
        hs = range(4 * g, 4 * g + 4)
        out.append(block_of(wq, rows(0, 4), sum((span(96 * h, 64) for h in hs), [])
                            + sum((span(96 * h + 64, 32) for h in hs), [])))
        out.append(block_of(wkv, rows(0, 2), sum((span(128 * h, 64) for h in hs), [])
                            + sum((span(128 * h + 64, 64) for h in hs), [])))
    cols_in(v["mla_w_out_2"][0], span(0, D))
    mlp(1)
    assert [o.size for o in out] == [P * k * w_ for _, k, w_ in PLAN]
    return np.concatenate(out)


def small_vectors(v):
    col = lambda q: np.asarray(q).reshape(-1, P).T
    zero = np.zeros((64, 64), np.float32)
    gates = []
    for w in (v["hy_ga_w_2"][0], v["hy_gx_w_2"][0]):
        for k in range(4):
            gates.append(np.block([[w[2 * k], zero], [zero, w[2 * k + 1]]]))
    parts = [col(v["c"]), col(v["ada_b"]), col(v["norm_pre"]), col(v["norm_post"]), col(v["pool_scale"]),
             col(v["hgrn_out_norm"]), col(v["hy_conv_w_2"]), col(v["hy_conv_b_2"]), col(v["hy_ga_b_2"]),
             col(v["hy_gx_b_2"]), col(v["hy_lambda_2"]), col(v["ln1_g_2"]), col(v["ln1_b_2"]), col(v["ln2_g_2"]),
             col(v["ln2_b_2"]), col(v["mla_q_norm_2"]), col(v["mla_kv_norm_2"]),
             np.concatenate(list(v["pool_w"][0]), axis=1), np.concatenate(gates, axis=1)]
    return np.ascontiguousarray(np.concatenate(parts, axis=1))


def constants():
    p, f = np.arange(P)[:, None], np.arange(P)[None, :]
    level = []
    for k in LEVELS:
        s_, t_ = p, f
        level.append(((s_ // (2 * k) == t_ // (2 * k)) & (s_ % (2 * k) < k) & (t_ % (2 * k) >= k)).astype(np.float32))
    t = np.arange(T)
    reset = np.broadcast_to((t % P != 0).astype(np.float32), (P, T))
    causal = np.where(f > p, np.float32(NEG), np.float32(0))
    delta = (t[None, :] - 384 - p).astype(np.float32)
    freq = 10000.0 ** (-np.arange(0, 32, 2, dtype=np.float32) / 32)
    ang = (t[None, :].astype(np.float32) * freq[np.arange(P) % 16][:, None].astype(np.float32)).astype(np.float32)
    perm = np.zeros((P, P), np.float32)
    for i in range(P):
        first = i % 32 < 16
        perm[i + 16 if first else i - 16, i] = -1.0 if first else 1.0
    inv = np.concatenate([np.broadcast_to(1.0 / np.minimum(np.arange(16) + 1, w), (P, 16)) for w in POOL_WINDOWS], 1)
    parts = [np.eye(P), np.ones((P, P)), perm, np.concatenate(level, 1), reset, causal, delta, np.cos(ang),
             np.sin(ang), inv]
    return np.ascontiguousarray(np.concatenate([np.asarray(q, np.float32) for q in parts], axis=1))


def bucket_rows():
    out = np.zeros((33, 3, BIAS_PITCH), np.float32)
    dist = 511 - np.arange(BIAS_PITCH)
    df = np.maximum(dist, 1).astype(np.float32)
    large = 16 + (np.log(df / np.float32(16)) / np.float32(np.log(2048 / 16)) * 16).astype(np.int32)
    bucket = np.where(dist < 16, np.maximum(dist, 0), np.minimum(large, 31))
    for g, dil in enumerate(DIL):
        seen = (dist >= 0) & (dist % dil == 0) & (dist <= 128 * dil)
        out[bucket[seen], g, np.nonzero(seen)[0]] = 1.0
        out[32, g, ~seen] = NEG
    return out.reshape(33, 3 * BIAS_PITCH)


STOP = 8


def kernel(**inputs):
    import concourse.bacc as bacc
    from concourse.bass_utils import run_bass_kernel_spmd

    v = {k: np.asarray(q) for k, q in inputs.items()}
    arrays = {
        "x": np.ascontiguousarray(v["x"][0].T.reshape(DC, P, T).transpose(1, 0, 2)),
        "w": weight_stream(v),
        "ada": np.concatenate([block_of(v["ada_w"][l, k], [P * c for c in range(DC)], slice(j, j + 256))
                               for l in range(2) for k in range(2) for j in range(0, 3 * D, 256)]),
        "vecs": small_vectors(v),
        "cst": constants(),
        "onehot": bucket_rows(),
        "relb": np.concatenate([v["rel_bias"], np.ones((1, 24), np.float32)]),
        "p": np.ascontiguousarray(v["p_2"][:, 0].transpose(0, 2, 1).reshape(2, 2, P, T).transpose(0, 2, 1, 3)),
    }
    nc = bacc.Bacc("TRN2", target_bir_lowering=False, num_devices=1)
    aps = {k: nc.dram_tensor(f"in_{k}", q.shape, mybir.dt.from_np(q.dtype), kind="ExternalInput").ap()
           for k, q in arrays.items()}
    out = nc.dram_tensor("out", (P, DC, T), F32, kind="ExternalOutput").ap()
    program(nc, aps, out, STOP)
    r = run_bass_kernel_spmd(nc, [{f"in_{k}": q for k, q in arrays.items()}], core_ids=[0])
    y = r.results[0]["out"]
    return np.ascontiguousarray(y.transpose(1, 0, 2).reshape(D, T).T)[None]
```
